# Optimizing a Trainium2 kernel written in Bass

```python
import math
import jax
import jax.numpy as jnp
from jax import lax
import numpy as np

D_MODEL = 1024
BATCH = 1
SEQ = 512
DEPTH = 2

N_ATTN_HEADS = 8
HEAD_DIM = 64
ATTN_WIDTH = N_ATTN_HEADS * HEAD_DIM
LRU_WIDTH = D_MODEL // 2
LRU_BLOCKS = 8
LRU_BLOCK = LRU_WIDTH // LRU_BLOCKS
LRU_CONV = 4
LRU_C = 8.0
CONV_WIDTH = D_MODEL // 2
CONV_KERNEL = 31
MOBA_BLOCK = 256
MOBA_TOPK = 3
MOBA_QCHUNK = 64
IDX_HEADS = 8
IDX_DIM = 64
DSA_TOPK_MAX = 256
DSA_QCHUNK = 128
REL_BUCKETS = 32
REL_MAX_EXACT = REL_BUCKETS // 2
REL_MAX_DIST = 128
D_FF = 2816
EPS = 1e-6
NEG = -1e30
EVEN_SPLITS = (LRU_WIDTH, LRU_WIDTH, ATTN_WIDTH, ATTN_WIDTH, ATTN_WIDTH)
ODD_SPLITS = (2 * CONV_WIDTH, ATTN_WIDTH, ATTN_WIDTH, ATTN_WIDTH, IDX_HEADS * IDX_DIM, IDX_DIM, IDX_HEADS)

kernel_name = 'hybrid_rglru_moba_conformer_dsa_macaron'

def _split(z, sizes):
    idx = list(np.cumsum(sizes)[:-1])
    return jnp.split(z, idx, axis=-1)

def rms_norm(x, g):
    xf = x.astype(jnp.float32)
    y = xf * lax.rsqrt(jnp.mean(xf * xf, axis=-1, keepdims=True) + EPS)
    return (y * g.astype(jnp.float32)).astype(x.dtype)

def layer_norm(x, g, b):
    xf = x.astype(jnp.float32)
    mu = jnp.mean(xf, axis=-1, keepdims=True)
    var = jnp.mean(jnp.square(xf - mu), axis=-1, keepdims=True)
    y = (xf - mu) * lax.rsqrt(var + EPS)
    return (y * g.astype(jnp.float32) + b.astype(jnp.float32)).astype(x.dtype)

def swiglu(x, w_gate, w_up, w_down):
    return (jax.nn.silu(x @ w_gate) * (x @ w_up)) @ w_down

def causal_depthwise_conv(x, w, b):
    width = w.shape[0]
    y = lax.conv_general_dilated(
        x, w[:, None, :].astype(x.dtype), window_strides=(1,), padding=[(width - 1, 0)],
        dimension_numbers=('NWC', 'WIO', 'NWC'), feature_group_count=x.shape[-1])
    return y + b.astype(x.dtype)

def rel_bucket(dist):
    n = jnp.maximum(dist, 0)
    nf = jnp.maximum(n, 1).astype(jnp.float32)
    large = REL_MAX_EXACT + (jnp.log(nf / REL_MAX_EXACT) / math.log(REL_MAX_DIST / REL_MAX_EXACT)
                             * (REL_BUCKETS - REL_MAX_EXACT)).astype(jnp.int32)
    large = jnp.minimum(large, REL_BUCKETS - 1)
    return jnp.where(n < REL_MAX_EXACT, n, large)

def head_rms(x, g):
    return rms_norm(x, g)

def _lru_combine(e1, e2):
    a1, b1 = e1
    a2, b2 = e2
    return a1 * a2, a2 * b1 + b2

def rg_lru(x, w_a, b_a, w_x, b_x, lam):
    bsz, seq, width = x.shape
    xb = x.reshape(bsz, seq, LRU_BLOCKS, LRU_BLOCK)
    r = jax.nn.sigmoid(jnp.einsum('bsgi,gij->bsgj', xb, w_a).reshape(bsz, seq, width) + b_a)
    i = jax.nn.sigmoid(jnp.einsum('bsgi,gij->bsgj', xb, w_x).reshape(bsz, seq, width) + b_x)
    log_a = -LRU_C * r.astype(jnp.float32) * jax.nn.softplus(-lam.astype(jnp.float32))
    a = jnp.exp(log_a)
    mult = jnp.sqrt(-jnp.expm1(2.0 * log_a))
    u = mult * (i * x).astype(jnp.float32)
    _, h = lax.associative_scan(_lru_combine, (a, u), axis=1)
    return h.astype(x.dtype)

def moba_attention(q, k, v, rel_bias):
    bsz, seq, nh, hd = q.shape
    nb = -(-seq // MOBA_BLOCK)
    pad = nb * MOBA_BLOCK - seq
    qh = q.transpose(0, 2, 1, 3)
    kh = jnp.pad(k.transpose(0, 2, 1, 3), ((0, 0), (0, 0), (0, pad), (0, 0)))
    vh = jnp.pad(v.transpose(0, 2, 1, 3), ((0, 0), (0, 0), (0, pad), (0, 0)))
    kblk = kh.reshape(bsz, nh, nb, MOBA_BLOCK, hd)
    vblk = vh.reshape(bsz, nh, nb, MOBA_BLOCK, hd)
    kmean = jnp.mean(kblk.astype(jnp.float32), axis=3).astype(k.dtype)
    topk = min(MOBA_TOPK, nb)
    scale = hd ** -0.5
    bidx = jnp.arange(bsz)[:, None, None, None]
    hidx = jnp.arange(nh)[None, :, None, None]
    h5 = jnp.arange(nh)[None, :, None, None, None]
    offs = jnp.arange(MOBA_BLOCK)
    blk_ids = jnp.arange(nb)

    def chunk(t0):
        qc = lax.dynamic_slice_in_dim(qh, t0, MOBA_QCHUNK, axis=2)
        t = t0 + jnp.arange(MOBA_QCHUNK)
        own = t0 // MOBA_BLOCK
        gate = jnp.einsum('bhcd,bhnd->bhcn', qc, kmean).astype(jnp.float32)
        gate = jnp.where(blk_ids < own, gate, NEG)
        _, sel = lax.top_k(gate, topk)
        valid = jnp.arange(topk) < own
        ksel = kblk[bidx, hidx, sel]
        vsel = vblk[bidx, hidx, sel]
        s_pos = sel[..., None] * MOBA_BLOCK + offs
        lsel = jnp.einsum('bhcd,bhcjsd->bhcjs', qc, ksel).astype(jnp.float32) * scale
        lsel = lsel + rel_bias[rel_bucket(t[None, None, :, None, None] - s_pos), h5].astype(jnp.float32)
        lsel = jnp.where(valid[:, None], lsel, NEG)
        kown = lax.dynamic_slice_in_dim(kh, own * MOBA_BLOCK, MOBA_BLOCK, axis=2)
        vown = lax.dynamic_slice_in_dim(vh, own * MOBA_BLOCK, MOBA_BLOCK, axis=2)
        s_own = own * MOBA_BLOCK + offs
        lown = jnp.einsum('bhcd,bhsd->bhcs', qc, kown).astype(jnp.float32) * scale
        lown = lown + rel_bias[rel_bucket(t[:, None] - s_own[None, :])].transpose(2, 0, 1).astype(jnp.float32)
        lown = jnp.where(s_own[None, :] <= t[:, None], lown, NEG)
        logits = jnp.concatenate([lsel.reshape(bsz, nh, MOBA_QCHUNK, topk * MOBA_BLOCK), lown], axis=-1)
        p = jax.nn.softmax(logits, axis=-1).astype(v.dtype)
        psel = p[..., :topk * MOBA_BLOCK].reshape(bsz, nh, MOBA_QCHUNK, topk, MOBA_BLOCK)
        pown = p[..., topk * MOBA_BLOCK:]
        return (jnp.einsum('bhcjs,bhcjsd->bhcd', psel, vsel)
                + jnp.einsum('bhcs,bhsd->bhcd', pown, vown))

    starts = jnp.arange(seq // MOBA_QCHUNK) * MOBA_QCHUNK
    outs = lax.map(chunk, starts)
    return outs.transpose(1, 0, 3, 2, 4).reshape(bsz, seq, nh * hd)

def dsa_attention(q, k, v, qi, ki, wi, rel_bias):
    bsz, seq, nh, hd = q.shape
    n_sel = min(DSA_TOPK_MAX, seq // 4)
    qchunk = min(DSA_QCHUNK, seq)
    scale = hd ** -0.5
    idx_scale = IDX_DIM ** -0.5 * IDX_HEADS ** -0.5
    bidx = jnp.arange(bsz)[:, None, None]
    key_pos = jnp.arange(seq)

    def chunk(t0):
        t = t0 + jnp.arange(qchunk)
        qic = lax.dynamic_slice_in_dim(qi, t0, qchunk, axis=1)
        wic = lax.dynamic_slice_in_dim(wi, t0, qchunk, axis=1)
        sc = jax.nn.relu(jnp.einsum('bchd,bsd->bchs', qic, ki).astype(jnp.float32))
        isc = jnp.einsum('bchs,bch->bcs', sc, wic.astype(jnp.float32)) * idx_scale
        isc = jnp.where(key_pos[None, None, :] <= t[None, :, None], isc, NEG)
        _, sel = lax.top_k(isc, n_sel)
        valid = sel <= t[None, :, None]
        ksel = k[bidx, sel]
        vsel = v[bidx, sel]
        qc = lax.dynamic_slice_in_dim(q, t0, qchunk, axis=1)
        logit = jnp.einsum('bchd,bckhd->bhck', qc, ksel).astype(jnp.float32) * scale
        bias = rel_bias[rel_bucket(t[None, :, None] - sel)].transpose(0, 3, 1, 2).astype(jnp.float32)
        logit = jnp.where(valid[:, None], logit + bias, NEG)
        p = jax.nn.softmax(logit, axis=-1).astype(v.dtype)
        return jnp.einsum('bhck,bckhd->bchd', p, vsel)

    starts = jnp.arange(seq // qchunk) * qchunk
    outs = lax.map(chunk, starts)
    return outs.transpose(1, 0, 2, 3, 4).reshape(bsz, seq, nh * hd)

def even_mixer(h, w_in, conv_w, conv_b, ra_w, ra_b, ix_w, ix_b, lam, q_norm, k_norm, w_out, rel_bias):
    bsz, seq, _ = h.shape
    gate, xr, q, k, v = _split(h @ w_in, EVEN_SPLITS)
    xr = causal_depthwise_conv(xr, conv_w, conv_b)
    ya = rg_lru(xr, ra_w, ra_b, ix_w, ix_b, lam) * jax.nn.gelu(gate)
    q = head_rms(q.reshape(bsz, seq, N_ATTN_HEADS, HEAD_DIM), q_norm)
    k = head_rms(k.reshape(bsz, seq, N_ATTN_HEADS, HEAD_DIM), k_norm)
    v = v.reshape(bsz, seq, N_ATTN_HEADS, HEAD_DIM)
    yb = moba_attention(q, k, v, rel_bias)
    return jnp.concatenate([ya, yb], axis=-1) @ w_out

def odd_mixer(h, w_in, dw_w, dw_b, ln_g, ln_b, q_norm, k_norm, w_out, rel_bias):
    bsz, seq, _ = h.shape
    glu, q, k, v, qi, ki, wi = _split(h @ w_in, ODD_SPLITS)
    ca, cg = jnp.split(glu, 2, axis=-1)
    c = ca * jax.nn.sigmoid(cg)
    c = causal_depthwise_conv(c, dw_w, dw_b)
    c = jax.nn.silu(layer_norm(c, ln_g, ln_b))
    q = head_rms(q.reshape(bsz, seq, N_ATTN_HEADS, HEAD_DIM), q_norm)
    k = head_rms(k.reshape(bsz, seq, N_ATTN_HEADS, HEAD_DIM), k_norm)
    v = v.reshape(bsz, seq, N_ATTN_HEADS, HEAD_DIM)
    qi = qi.reshape(bsz, seq, IDX_HEADS, IDX_DIM)
    yd = dsa_attention(q, k, v, qi, ki, wi, rel_bias)
    return jnp.concatenate([c, yd], axis=-1) @ w_out

def setup_inputs(seed: int = 0) -> dict:
    key = jax.random.key(seed)
    ks = iter(jax.random.split(key, 40))
    n_even = (DEPTH + 1) // 2
    n_odd = DEPTH // 2

    def nrm(shape, fan_in):
        return jax.random.normal(next(ks), shape, jnp.float32) * fan_in ** -0.5

    def gain(shape):
        return 1.0 + 0.02 * jax.random.normal(next(ks), shape, jnp.float32)

    def bias(shape):
        return 0.01 * jax.random.normal(next(ks), shape, jnp.float32)

    x = jax.random.normal(next(ks), (BATCH, SEQ, D_MODEL), jnp.float32)
    rel_bias = 0.2 * jax.random.normal(next(ks), (REL_BUCKETS, N_ATTN_HEADS), jnp.float32)
    ffn1_norm = gain((DEPTH, D_MODEL))
    ffn1_w_gate = nrm((DEPTH, D_MODEL, D_FF), D_MODEL)
    ffn1_w_up = nrm((DEPTH, D_MODEL, D_FF), D_MODEL)
    ffn1_w_down = nrm((DEPTH, D_FF, D_MODEL), D_FF)
    mix_norm = gain((DEPTH, D_MODEL))
    ffn2_norm = gain((DEPTH, D_MODEL))
    ffn2_w_gate = nrm((DEPTH, D_MODEL, D_FF), D_MODEL)
    ffn2_w_up = nrm((DEPTH, D_MODEL, D_FF), D_MODEL)
    ffn2_w_down = nrm((DEPTH, D_FF, D_MODEL), D_FF)
    ev_w_in = nrm((n_even, D_MODEL, sum(EVEN_SPLITS)), D_MODEL)
    ev_conv_w = nrm((n_even, LRU_CONV, LRU_WIDTH), LRU_CONV)
    ev_conv_b = bias((n_even, LRU_WIDTH))
    ev_ra_w = nrm((n_even, LRU_BLOCKS, LRU_BLOCK, LRU_BLOCK), LRU_BLOCK)
    ev_ra_b = bias((n_even, LRU_WIDTH))
    ev_ix_w = nrm((n_even, LRU_BLOCKS, LRU_BLOCK, LRU_BLOCK), LRU_BLOCK)
    ev_ix_b = bias((n_even, LRU_WIDTH))
    a0 = jax.random.uniform(next(ks), (n_even, LRU_WIDTH), jnp.float32, 0.9, 0.999)
    s = a0 ** (1.0 / LRU_C)
    ev_lambda = jnp.log(s) - jnp.log1p(-s)
    ev_q_norm = gain((n_even, HEAD_DIM))
    ev_k_norm = gain((n_even, HEAD_DIM))
    ev_w_out = nrm((n_even, LRU_WIDTH + ATTN_WIDTH, D_MODEL), LRU_WIDTH + ATTN_WIDTH)
    od_w_in = nrm((n_odd, D_MODEL, sum(ODD_SPLITS)), D_MODEL)
    od_dw_w = nrm((n_odd, CONV_KERNEL, CONV_WIDTH), CONV_KERNEL)
    od_dw_b = bias((n_odd, CONV_WIDTH))
    od_ln_g = gain((n_odd, CONV_WIDTH))
    od_ln_b = bias((n_odd, CONV_WIDTH))
    od_q_norm = gain((n_odd, HEAD_DIM))
    od_k_norm = gain((n_odd, HEAD_DIM))
    od_w_out = nrm((n_odd, CONV_WIDTH + ATTN_WIDTH, D_MODEL), CONV_WIDTH + ATTN_WIDTH)
    return {
        'x': x, 'rel_bias': rel_bias,
        'ffn1_norm': ffn1_norm, 'ffn1_w_gate': ffn1_w_gate, 'ffn1_w_up': ffn1_w_up, 'ffn1_w_down': ffn1_w_down,
        'mix_norm': mix_norm,
        'ffn2_norm': ffn2_norm, 'ffn2_w_gate': ffn2_w_gate, 'ffn2_w_up': ffn2_w_up, 'ffn2_w_down': ffn2_w_down,
        'ev_w_in': ev_w_in, 'ev_conv_w': ev_conv_w, 'ev_conv_b': ev_conv_b, 'ev_ra_w': ev_ra_w, 'ev_ra_b': ev_ra_b,
        'ev_ix_w': ev_ix_w, 'ev_ix_b': ev_ix_b, 'ev_lambda': ev_lambda, 'ev_q_norm': ev_q_norm,
        'ev_k_norm': ev_k_norm, 'ev_w_out': ev_w_out,
        'od_w_in': od_w_in, 'od_dw_w': od_dw_w, 'od_dw_b': od_dw_b, 'od_ln_g': od_ln_g, 'od_ln_b': od_ln_b,
        'od_q_norm': od_q_norm, 'od_k_norm': od_k_norm, 'od_w_out': od_w_out,
    }

def reference(x, rel_bias,
              ffn1_norm, ffn1_w_gate, ffn1_w_up, ffn1_w_down,
              mix_norm,
              ffn2_norm, ffn2_w_gate, ffn2_w_up, ffn2_w_down,
              ev_w_in, ev_conv_w, ev_conv_b, ev_ra_w, ev_ra_b, ev_ix_w, ev_ix_b, ev_lambda,
              ev_q_norm, ev_k_norm, ev_w_out,
              od_w_in, od_dw_w, od_dw_b, od_ln_g, od_ln_b, od_q_norm, od_k_norm, od_w_out):
    for i in range(DEPTH):
        h = rms_norm(x, ffn1_norm[i])
        x = x + 0.5 * swiglu(h, ffn1_w_gate[i], ffn1_w_up[i], ffn1_w_down[i])
        h = rms_norm(x, mix_norm[i])
        j = i // 2
        if i % 2 == 0:
            x = x + even_mixer(h, ev_w_in[j], ev_conv_w[j], ev_conv_b[j], ev_ra_w[j], ev_ra_b[j],
                               ev_ix_w[j], ev_ix_b[j], ev_lambda[j], ev_q_norm[j], ev_k_norm[j],
                               ev_w_out[j], rel_bias)
        else:
            x = x + odd_mixer(h, od_w_in[j], od_dw_w[j], od_dw_b[j], od_ln_g[j], od_ln_b[j],
                              od_q_norm[j], od_k_norm[j], od_w_out[j], rel_bias)
        h = rms_norm(x, ffn2_norm[i])
        x = x + 0.5 * swiglu(h, ffn2_w_gate[i], ffn2_w_up[i], ffn2_w_down[i])
    return x


_drawn_inputs = setup_inputs


def setup_inputs(seed=0):
    import zlib

    import numpy as np

    out = dict(_drawn_inputs(seed))
    spreads = {}
    factors = {'ffn1_norm': 3.775,
     'mix_norm': 3.387,
     'ffn2_norm': 4.449,
     'ev_ra_b': 8.0,
     'ev_ix_b': 8.0,
     'ev_q_norm': 8.0,
     'ev_k_norm': 8.0,
     'od_dw_b': 8.0,
     'od_ln_g': 6.632,
     'od_ln_b': 8.0,
     'od_q_norm': 8.0,
     'od_k_norm': 8.0}
    for name, (base, spread) in spreads.items():
        noise = np.random.default_rng([zlib.crc32(name.encode()), seed]).standard_normal(out[name].shape)
        drawn = base * np.exp(spread * noise) if base else spread * noise
        out[name] = jnp.asarray(drawn.astype(out[name].dtype))
    for name, factor in factors.items():
        out[name] = (out[name] * factor).astype(out[name].dtype)
    return out
```

```python
from contextlib import ExitStack

import numpy as np

import concourse.bass as bass
from concourse import mybir

F32 = mybir.dt.float32
F32R = mybir.dt.float32r
ALU = mybir.AluOpType
ACT = mybir.ActivationFunctionType
AX_X = mybir.AxisListType.X
ds = bass.ds

P = 128
T = 512
TT = T // P
D = 1024
KT = D // P
DFF = 2816
FT = DFF // P
GROUPS = (8, 8, 6)
UNIT = KT * P
RAW = 4
EPS = 1e-6
NEG = -1e30
HEADS = 8
HD = 64
BUCKETS = 32
TAPS = 4
DW_TAPS = 31
LRU_C = 8.0
ARENA = 6560
SKEW = 640

FFN_UNITS = 2 * FT + len(GROUPS) * KT
MIX_IN = 20
IDX_IN = 5
EVEN_UNITS = MIX_IN + KT
ODD_UNITS = IDX_IN + MIX_IN + KT
PHASES = ("ffn", "even", "ffn", "ffn", "odd", "ffn")
PHASE_UNITS = {"ffn": FFN_UNITS, "even": EVEN_UNITS, "odd": ODD_UNITS}
UNIT_BASE = [sum(PHASE_UNITS[p] for p in PHASES[:i]) for i in range(len(PHASES) + 1)]
NUNITS = UNIT_BASE[-1]
X_UPDATES = {"ffn": len(GROUPS) * KT, "even": 0, "odd": 0}
X_BASE = [sum(X_UPDATES[p] for p in PHASES[:i]) for i in range(len(PHASES) + 1)]
FFN_BASE = [FT * PHASES[:i].count("ffn") for i in range(len(PHASES) + 1)]

VEC_SIZES = (("norm", len(PHASES) * KT), ("conv_w", 4 * TAPS), ("conv_b", 4), ("ra_b", 4), ("ix_b", 4),
             ("lam", 4), ("ev_q", 1), ("ev_k", 1), ("dw_w", 4 * DW_TAPS), ("dw_b", 4), ("ln_g", 4),
             ("ln_b", 4), ("od_q", 1), ("od_k", 1))
COL = {}
NVEC = 0
for _name, _n in VEC_SIZES:
    COL[_name] = NVEC
    NVEC += _n


def build(nc, xt_in, w_stream, vec_in, bd_in, relb_in, onehot_in, ident_in, out):
    with ExitStack() as ctx:
        top = [(nc.sbuf_base + 31) // 32 * 32]

        def sb(name, shape, dt=F32, at=None):
            size = int(np.prod(shape[1:])) * 4
            if at is None:
                at, top[0] = top[0], top[0] + (size + 31) // 32 * 32
            return nc.alloc_sbuf_tensor_at(name, shape, dt, offset=at)

        def sem(name):
            return ctx.enter_context(nc.semaphore(name))

        xt = sb("xt", [P, KT * T])
        xs_hi = sb("xs_hi", [P, KT, T], F32R)
        xs_lo = sb("xs_lo", [P, KT, T], F32R)
        raw = sb("raw", [P, RAW, UNIT])
        w_hi = sb("w_hi", [P, 2, UNIT], F32R)
        w_lo = sb("w_lo", [P, 2, UNIT], F32R)
        a_hi = sb("a_hi", [P, 8 * T], F32R)
        gelu_1_at = top[0] + 7 * T * 4
        a_lo = sb("a_lo", [P, 8 * T], F32R)
        vec = sb("vec", [P, NVEC])
        ident = sb("ident", [P, P])
        ones = sb("ones", [P, P])
        small = sb("small", [P, 8])
        rcol = sb("rcol", [P, TT])
        rstd = sb("rstd", [P, T])
        half = sb("half", [P, T])
        t0 = sb("t0", [P, T])
        t1 = sb("t1", [P, T])
        t2 = sb("t2", [P, T])
        sqb = sb("sqb", [P, 2, T])
        acc = sb("acc", [P, T])
        diag = sb("diag", [P, T])

        bias_t = sb("bias_t", [P, HEADS, T])
        gq8 = sb("gq8", [P, 2])
        head_sel = sb("head_sel", [P, 2])
        head_row = sb("head_row", [P, 3 * HD])
        q_hi = sb("q_hi", [P, 2, T], F32R)
        q_lo = sb("q_lo", [P, 2, T], F32R)
        k_hi = sb("k_hi", [P, 2, T], F32R)
        k_lo = sb("k_lo", [P, 2, T], F32R)
        v_hi = sb("v_hi", [P, 2, TT, 3 * HD], F32R)
        v_lo = sb("v_lo", [P, 2, TT, 3 * HD], F32R)
        hstd = sb("hstd", [P, 16])
        hinv = sb("hinv", [P, 2, 16])
        probs = sb("probs", [P, 2, T])
        rowmax = sb("rowmax", [P, 2])
        negmax = sb("negmax", [P, 2])
        rowsum = sb("rowsum", [P, 2])
        rowinv = sb("rowinv", [P, 2])
        pt_hi = sb("pt_hi", [P, TT, T], F32R)
        pt_lo = sb("pt_lo", [P, TT, T], F32R)
        shared = top[0]
        bdr_hi = sb("bdr_hi", [P, 2, 4, P], F32R)
        bdr_lo = sb("bdr_lo", [P, 2, 4, P], F32R)
        xc_hi = sb("xc_hi", [P, T], F32R)
        xc_lo = sb("xc_lo", [P, T], F32R)
        c8 = sb("c8", [P, 8])[:, :]
        sp = sb("sp", [P, 16])[:, :]
        xr_pad = sb("xr_pad", [P, T + TAPS])[:, :]
        xc = sb("xc", [P, T])[:, :]
        gelu = [sb("gelu_0", [P, T])[:, :], sb("gelu_1", [P, T], at=gelu_1_at)[:, :]]
        ra = sb("ra", [P, T])[:, :]
        ri = sb("ri", [P, T])[:, :]
        hh = sb("hh", [P, T])[:, :]
        even_top = top[0]
        top[0] = shared
        causal = sb("causal", [P, P])[:, :]
        isc = sb("isc", [P, P * (2 + 3 + 4)])[:, :]
        top8 = sb("top8", [P, 8])[:, :]
        wi = sb("wi", [P, TT * HEADS])[:, :]
        relu = [probs[:, 0, :], probs[:, 1, :]]
        c_pad = [sb(f"c_pad{j}", [P, T + DW_TAPS - 1])[:, :] for j in range(4)]
        cv = [sb(f"cv{j}", [P, T])[:, :] for j in range(4)]
        ki_hi = sb("ki_hi", [P, T], F32R)
        ki_lo = sb("ki_lo", [P, T], F32R)
        squares = [sqb[:, 0, :], sqb[:, 1, :], t0[:, :], t1[:, :]]
        odd_top = top[0]
        top[0] = shared + 2 * 4 * UNIT
        table = sb("table", [HEADS, SKEW])[:, :]
        relb = sb("relb", [BUCKETS, HEADS])[:, :]
        onehot = sb("onehot", [BUCKETS, T])[:, :]
        bd_raw = sb("bd_raw", [P, UNIT])[:, :]
        assert max(even_top, odd_top, top[0]) <= nc.sbuf_usable_end, (even_top, odd_top)
        skew = nc.dram_tensor("skew", [HEADS, P, SKEW], F32).ap()

        ps_s = ctx.enter_context(nc.psum_tensor("ps_s", [P, 2, T], F32))
        ps_t = ctx.enter_context(nc.psum_tensor("ps_t", [P, 2, T], F32))
        ps_unit = ctx.enter_context(nc.psum_tensor("ps_unit", [P, 2, T], F32))
        ps_misc = ctx.enter_context(nc.psum_tensor("ps_misc", [P, T], F32))
        ps_y = ctx.enter_context(nc.psum_tensor("ps_y", [P, T], F32))

        w_landed = [sem(f"w_landed{s}") for s in range(RAW)]
        w_hi_done = sem("w_hi_done")
        w_lo_done = sem("w_lo_done")
        unit_done = sem("unit_done")
        unit_read = sem("unit_read")
        silu_done = sem("silu_done")
        a_hi_done = sem("a_hi_done")
        a_lo_done = sem("a_lo_done")
        x_landed = sem("x_landed")
        c_landed = sem("c_landed")
        x_added = sem("x_added")
        x_hi_done = sem("x_hi_done")
        x_lo_done = sem("x_lo_done")
        sq_done = sem("sq_done")
        acc_done = sem("acc_done")
        ssq_done = sem("ssq_done")
        std_done = sem("std_done")
        rcol_done = sem("rcol_done")
        diag_done = sem("diag_done")
        rbc_done = sem("rbc_done")
        rstd_done = sem("rstd_done")
        half_done = sem("half_done")
        const_done = sem("const_done")
        q_sq_done = sem("q_sq_done")
        k_sq_done = sem("k_sq_done")
        q_hi_done = sem("q_hi_done")
        q_lo_done = sem("q_lo_done")
        k_hi_done = sem("k_hi_done")
        k_lo_done = sem("k_lo_done")
        v_hi_done = sem("v_hi_done")
        v_lo_done = sem("v_lo_done")
        hssq_done = sem("hssq_done")
        hstd_done = sem("hstd_done")
        hinv_done = sem("hinv_done")
        kdiag_done = sem("kdiag_done")
        kn_done = sem("kn_done")
        kbc_done = sem("kbc_done")
        vt_done = sem("vt_done")
        score_done = sem("score_done")
        biased_done = sem("biased_done")
        masked_done = sem("masked_done")
        rowmax_done = sem("rowmax_done")
        negmax_done = sem("negmax_done")
        exp_done = sem("exp_done")
        rowinv_done = sem("rowinv_done")
        prob_done = sem("prob_done")
        turned_done = sem("turned_done")
        pt_hi_done = sem("pt_hi_done")
        pt_lo_done = sem("pt_lo_done")
        pv_done = sem("pv_done")
        y_hi_done = sem("y_hi_done")
        y_lo_done = sem("y_lo_done")
        bd_hi_done = sem("bd_hi_done")
        bd_lo_done = sem("bd_lo_done")
        pad_done = sem("pad_done")
        conv_done = sem("conv_done")
        xc_hi_done = sem("xc_hi_done")
        xc_lo_done = sem("xc_lo_done")
        gelu_done = sem("gelu_done")
        gate_r_done = sem("gate_r_done")
        gate_i_done = sem("gate_i_done")
        sig_r_done = sem("sig_r_done")
        sig_i_done = sem("sig_i_done")
        tanh_done = sem("tanh_done")
        decay_done = sem("decay_done")
        sqa_done = sem("sqa_done")
        ix_done = sem("ix_done")
        mult2_done = sem("mult2_done")
        mult_done = sem("mult_done")
        u_done = sem("u_done")
        scan_done = sem("scan_done")
        ly_done = sem("ly_done")
        l_hi_done = sem("l_hi_done")
        l_lo_done = sem("l_lo_done")
        sp_done = sem("sp_done")
        spe_done = sem("spe_done")
        table_mm = sem("table_mm")
        table_done = sem("table_done")
        skewed = sem("skewed")
        bias_landed = sem("bias_landed")
        wi_turned = sem("wi_turned")
        wi_done = sem("wi_done")
        ki_hi_done = sem("ki_hi_done")
        ki_lo_done = sem("ki_lo_done")
        ki_landed = sem("ki_landed")
        idx_done = sem("idx_done")
        relu_done = sem("relu_done")
        isc_done = sem("isc_done")
        top_done = sem("top_done")
        cut_done = sem("cut_done")
        sel_done = sem("sel_done")
        qi_hi_done = sem("qi_hi_done")
        qi_lo_done = sem("qi_lo_done")
        glu_sig_done = sem("glu_sig_done")
        glu_done = sem("glu_done")
        dw_done = sem("dw_done")
        mean_mm = sem("mean_mm")
        ln_add_done = sem("ln_add_done")
        cen_done = sem("cen_done")
        cen_sq_done = sem("cen_sq_done")
        var_mm = sem("var_mm")
        ln_std_done = sem("ln_std_done")
        ln_rcol_done = sem("ln_rcol_done")
        ln_diag_done = sem("ln_diag_done")
        ln_bc_done = sem("ln_bc_done")
        scaled_done = sem("scaled_done")
        cy_done = sem("cy_done")
        ln_chain = sem("ln_chain")
        gq_done = sem("gq_done")
        causal_done = sem("causal_done")
        stored = sem("stored")

        block = ctx.enter_context(nc.Block())

        def xt_tile(d):
            return xt[:, ds(d * T, T)]

        def gain(col, d):
            return vec[:, ds(COL[col] + d, 1)]

        @block.sync
        def _(sp):
            def load(n, slot):
                sp.dma_start(raw[:, slot, :], w_stream[ds(n, 1), :, :].rearrange("a p c -> (a p) c")).then_inc(w_landed[slot], 16)

            for n in range(RAW):
                load(n, n)
            with sp.Fori(1, NUNITS // RAW) as i:
                for s in range(RAW):
                    sp.wait_ge(w_lo_done, i * RAW + (s - RAW + 1))
                    load(i * RAW + s, s)
            for n in range(NUNITS // RAW * RAW, NUNITS):
                sp.wait_ge(w_lo_done, n - RAW + 1)
                load(n, n % RAW)
            for d in range(KT):
                sp.wait_ge(x_added, X_BASE[-1] - KT + d + 1)
                sp.dma_start(out[d], xt_tile(d)).then_inc(stored, 16)
            sp.wait_ge(stored, 16 * KT)

        @block.gpsimd
        def _(pool):
            def constant(n, out, value):
                nc.gpsimd.memset(out, value).then_inc(const_done, 1)
                pool.wait_ge(const_done, n)

            constant(1, ones[:, :], 1.0)
            constant(2, small[:, 0:1], EPS)
            constant(3, table[:, T:SKEW], NEG)
            constant(4, head_sel[:, :], 0.0)
            constant(5, head_row[:, :], 0.0)
            constant(6, head_row[:, HD:2 * HD], 1.0)
            for h in range(2):
                constant(7 + h, head_sel[h * HD:(h + 1) * HD, h:h + 1], 1.0)
            for b, buf in enumerate((v_hi, v_lo)):
                for par in range(2):
                    constant(9 + 2 * b + par, buf[:, par, :, HD:2 * HD].bitcast(F32), 0.0)
            if "odd" in PHASES:
                pool.wait_ge(unit_done, UNIT_BASE[PHASES.index("odd")])
                pool.wait_ge(unit_read, UNIT_BASE[PHASES.index("odd")])
                nc.gpsimd.memset(causal, 0.0).then_inc(causal_done, 1)
                pool.wait_ge(causal_done, 1)
                nc.gpsimd.affine_select(out=causal, in_=causal, compare_op=ALU.is_ge, fill=NEG, base=0,
                                        pattern=[[-1, P]], channel_multiplier=1).then_inc(causal_done, 1)

        @block.tensor
        def _(pe):
            def product(ps, lhs_hi, lhs_lo, rhs_hi, rhs_lo, first, last):
                pe.matmul(ps, lhs_hi, rhs_hi, start=first, stop=False)
                pe.matmul(ps, lhs_hi, rhs_lo, start=False, stop=False)
                return pe.matmul(ps, lhs_lo, rhs_hi, start=False, stop=last)

            def start_unit(n, is_first=False):
                pe.wait_ge(w_lo_done, n + 1)
                if not is_first:
                    pe.wait_ge(unit_read, n - 1)

            def blocks(s, ks, rhs_hi, rhs_lo, nk=KT, wait=None):
                for k in ks:
                    if wait:
                        wait(k)
                    w = slice(k * P, (k + 1) * P)
                    mm = product(ps_unit[:, s, :], w_hi[:, s, w], w_lo[:, s, w], rhs_hi(k), rhs_lo(k),
                                 k == 0, k == nk - 1)
                return mm

            def of_x(hi):
                return (lambda k: xs_hi[:, k, :]) if hi else (lambda k: xs_lo[:, k, :])

            def of_a(hi):
                buf = a_hi if hi else a_lo
                return lambda k: buf[:, k * T:(k + 1) * T]

            def first_units(i):
                n = UNIT_BASE[i]
                start_unit(n, is_first=n < 2)
                blocks(n % 2, range(KT), of_x(1), of_x(0),
                       wait=lambda k: pe.wait_ge(x_lo_done, KT * i + k + 1)).then_inc(unit_done, 1)
                pe.wait_ge(const_done, 2)
                pe.wait_ge(acc_done, KT * (i + 1))
                for t in range(TT):
                    mm = pe.matmul(ps_misc[:, t:t + 1], acc[:, t * P:(t + 1) * P], ones[:, 0:1], start=True, stop=True)
                mm.then_inc(ssq_done, 1)
                n += 1
                start_unit(n, is_first=n < 2)
                blocks(n % 2, range(KT // 2), of_x(1), of_x(0))
                pe.wait_ge(diag_done, i + 1)
                pe.matmul(ps_misc[:, :], ones[:, :], diag[:, :], start=True, stop=True).then_inc(rbc_done, 1)
                blocks(n % 2, range(KT // 2, KT), of_x(1), of_x(0)).then_inc(unit_done, 1)

            def x_unit(n, s):
                start_unit(n)
                blocks(s, range(KT), of_x(1), of_x(0)).then_inc(unit_done, 1)

            def ffn(i):
                n0, tile0 = UNIT_BASE[i], FFN_BASE[i]
                first_units(i)
                for k in (2, 3):
                    x_unit(n0 + k, (n0 + k) % 2)
                n, tile = n0, tile0
                for g, tiles in enumerate(GROUPS):
                    with pe.Fori(1 if g == 0 else 0, tiles // 2) as it:
                        for k in range(4):
                            x_unit(it * 4 + (n + k), (n0 + k) % 2)
                    n, tile = n + 2 * tiles, tile + tiles
                    with pe.Fori(0, KT // 4) as it:
                        for k in range(4):
                            start_unit(it * 4 + (n + k))
                            blocks((n0 + k) % 2, range(tiles), of_a(1), of_a(0), nk=tiles,
                                   wait=lambda f: pe.wait_ge(a_lo_done, tile - tiles + f + 1) if k == 0 else None
                                   ).then_inc(unit_done, 1)
                    n += KT


            def mix_first(i):
                first_units(i)

            def head_ssq(a):
                pe.wait_ge(q_sq_done, a + 1)
                pe.wait_ge(k_sq_done, a + 1)
                if a:
                    pe.wait_ge(kn_done, a)
                for m in range(2):
                    for t in range(TT):
                        mm = pe.matmul(ps_misc[:, (m * TT + t) * 2:(m * TT + t) * 2 + 2],
                                       sqb[:, m, t * P:(t + 1) * P], head_sel[:, :], start=True, stop=True)
                mm.then_inc(hssq_done, 1)

            def turn_v(a, n):
                pe.wait_ge(unit_read, n + 1)
                pe.wait_ge(hstd_done, a + 1)
                for t in range(TT):
                    mm = pe.transpose(ps_misc[:, t * P:(t + 1) * P], t2[:, t * P:(t + 1) * P], ident[:, :])
                mm.then_inc(vt_done, 1)

            def spread_k(a):
                pe.wait_ge(kdiag_done, a + 1)
                pe.wait_ge(v_lo_done, a + 1)
                pe.matmul(ps_misc[:, :], head_row[:, HD:3 * HD], diag[:, :], start=True, stop=False)
                pe.matmul(ps_misc[:, :], head_row[:, 0:2 * HD], acc[:, :], start=False, stop=True).then_inc(kbc_done, 1)

            def score(a, r):
                R, h, n = 8 * a + r, r // 4, (r % 4 + 1) * P
                if r == 0:
                    pe.wait_ge(k_lo_done, a + 1)
                    pe.wait_ge(q_lo_done, a + 1)
                if R >= 2:
                    pe.wait_ge(biased_done, R - 1)
                f, t = slice(h * HD, (h + 1) * HD), slice(n - P, n)
                product(ps_s[:, R % 2, 0:n], q_hi[f, a % 2, t], q_lo[f, a % 2, t], k_hi[f, a % 2, 0:n],
                        k_lo[f, a % 2, 0:n], True, True).then_inc(score_done, 1)

            def turn(a, r):
                R = 8 * a + r
                pe.wait_ge(prob_done, R + 1)
                if R >= 2:
                    pe.wait_ge(pt_lo_done, R - 1)
                for j in range(r % 4 + 1):
                    mm = pe.transpose(ps_t[:, R % 2, j * P:(j + 1) * P], probs[:, R % 2, j * P:(j + 1) * P], ident[:, :])
                mm.then_inc(turned_done, 1)

            def weigh(a, h):
                pe.wait_ge(pt_lo_done, 8 * a + 4 * h + 4)
                if h == 0 and a < 4:
                    pe.wait_ge(sig_i_done, a + 1)
                elif h == 0:
                    pe.wait_ge(y_lo_done, a)
                for j in range(TT):
                    w = slice(h * HD, h * HD + P)
                    mm = product(ps_y[:, j * P:T], v_hi[:, a % 2, j, w], v_lo[:, a % 2, j, w],
                                 pt_hi[:, j, j * P:T], pt_lo[:, j, j * P:T], h == 0 and j == 0, h == 1 and j == TT - 1)
                mm.then_inc(pv_done, 1)

            def attend(a, p, first):
                if p == 0 and not first:
                    weigh(a - 1, 1)
                if p == 3:
                    weigh(a, 0)
                for r in (2 * p - 2, 2 * p - 1):
                    if r >= 0:
                        turn(a, r)
                if p < 4:
                    score(a, 2 * p)
                    score(a, 2 * p + 1)

            def lru_gate(j, which):
                if which == 0:
                    pe.wait_ge(xc_lo_done, j + 1)
                    if j:
                        pe.wait_ge(y_lo_done, j)
                    pe.wait_ge(bd_lo_done, 1)
                else:
                    pe.wait_ge(sig_r_done, j + 1)
                product(ps_y[:, :], bdr_hi[:, which, j, :], bdr_lo[:, which, j, :], xc_hi[:, :], xc_lo[:, :],
                        True, True).then_inc(gate_r_done if which == 0 else gate_i_done, 1)

            def out_blocks(n, s, ks, first, last):
                for k in ks:
                    w = slice(k * P, (k + 1) * P)
                    y = slice(k * T, (k + 1) * T)
                    mm = product(ps_unit[:, s, :], w_hi[:, s, w], w_lo[:, s, w], a_hi[:, y], a_lo[:, y],
                                 first and k == ks[0], last and k == ks[-1])
                return mm

            def mix_out(i, n, a0, early, late, wait_branch, wait_late):
                for u in range(5):
                    if PHASES[i] == "even" and u in (1, 2):
                        lru_gate(3, u - 1)
                    attend(a0 + 3, u, False)
                    if u < 2:
                        start_unit(n + u)
                        if u == 0:
                            wait_branch()
                        out_blocks(n + u, (n + u) % 2, early[:-1], True, False)
                        pe.wait_ge(y_lo_done, a0 + 3)
                        out_blocks(n + u, (n + u) % 2, early[-1:], False, False)
                weigh(a0 + 3, 1)
                wait_late()
                pe.wait_ge(y_lo_done, a0 + 4)
                for u in range(KT):
                    if u >= 2:
                        start_unit(n + u)
                        out_blocks(n + u, (n + u) % 2, early, True, False)
                    out_blocks(n + u, (n + u) % 2, late, False, True).then_inc(unit_done, 1)

            def even(i):
                n0 = UNIT_BASE[i]
                for it in range(4):
                    for u in range(5):
                        n = n0 + 5 * it + u
                        if it == 0 and u == 0:
                            first_units(i)
                        elif it or u > 1:
                            x_unit(n, n % 2)
                        if it:
                            if u == 1:
                                lru_gate(it - 1, 0)
                            if u == 2:
                                lru_gate(it - 1, 1)
                            attend(it - 1, u, it == 1)
                        if u == 2:
                            head_ssq(it)
                        if u == 3:
                            turn_v(it, n0 + 5 * it + 2)
                        if u == 4:
                            spread_k(it)
                mix_out(i, n0 + MIX_IN, 0, (4, 5, 0, 1, 2, 6), (3, 7), lambda: pe.wait_ge(l_lo_done, 3),
                        lambda: pe.wait_ge(l_lo_done, 4))

            def index_row(q):
                t, h = 1 + q // HEADS, q % HEADS
                n = (t + 1) * P
                if q == 0:
                    pe.wait_ge(qi_lo_done, 4)
                    pe.wait_ge(ki_landed, 32)
                if q >= 2:
                    pe.wait_ge(relu_done, q - 1)
                else:
                    pe.wait_ge(biased_done, 32)
                f = slice(h % 2 * HD, h % 2 * HD + HD)
                qi = slice((4 + h // 2) * T + t * P, (4 + h // 2) * T + (t + 1) * P)
                product(ps_s[:, q % 2, 0:n], a_hi[f, qi], a_lo[f, qi], ki_hi[f, 0:n], ki_lo[f, 0:n],
                        True, True).then_inc(idx_done, 1)

            def odd(i):
                n0 = UNIT_BASE[i]
                first_units(i)
                for u in range(2, IDX_IN):
                    x_unit(n0 + u, (n0 + u) % 2)
                pe.wait_ge(unit_read, n0 + 1)
                pe.wait_ge(rstd_done, i + 1)
                for t in range(TT):
                    mm = pe.transpose(ps_misc[:, t * P:(t + 1) * P], t0[:, t * P:(t + 1) * P], ident[:, :])
                mm.then_inc(wi_turned, 1)
                for m in range(8):
                    x_unit(n0 + IDX_IN + m, (n0 + IDX_IN + m) % 2)
                    if m < 4:
                        for q in range(6 * m, 6 * m + 6):
                            index_row(q)
                for it in range(4):
                    for u in range(5):
                        if u < 3:
                            n = n0 + IDX_IN + 8 + 3 * it + u
                            x_unit(n, n % 2)
                        if it:
                            attend(4 + it - 1, u, it == 1)
                        if u == 2:
                            head_ssq(4 + it)
                        if u == 3:
                            turn_v(4 + it, n0 + IDX_IN + 8 + 3 * it + 2)
                        if u == 4:
                            spread_k(4 + it)
                mix_out(i, n0 + IDX_IN + MIX_IN, 4, (4, 5, 6), (0, 1, 2, 3, 7), lambda: None, conv_norm)

            def conv_norm():
                pe.wait_ge(ln_add_done, 1)
                pe.matmul(ps_misc[:, :], ones[:, :], acc[:, :], start=True, stop=True).then_inc(mean_mm, 1)
                pe.wait_ge(ln_add_done, 2)
                for t in range(TT):
                    mm = pe.matmul(ps_misc[:, t:t + 1], acc[:, t * P:(t + 1) * P], ones[:, 0:1], start=True, stop=True)
                mm.then_inc(var_mm, 1)
                pe.wait_ge(ln_diag_done, 1)
                pe.matmul(ps_misc[:, :], ones[:, :], diag[:, :], start=True, stop=True).then_inc(ln_bc_done, 1)
                pe.wait_ge(l_lo_done, 8)

            pe.wait_ge(c_landed, 16 * 5)
            pe.matmul(ps_y[0:HEADS, :], relb, onehot, start=True, stop=True).then_inc(table_mm, 1)
            for i, phase in enumerate(PHASES):
                {"ffn": ffn, "even": even, "odd": odd}[phase](i)

        @block.scalar
        def _(act):
            def split_hi(n, slot, s, is_first=False):
                act.wait_ge(w_landed[slot], 16 * (n // RAW + 1) if type(n) is int else (n - slot) * (16 // RAW) + 16)
                if not is_first:
                    act.wait_ge(unit_done, n - 1)
                act.activation(w_hi[:, s, :], raw[:, slot, :], ACT.Copy).then_inc(w_hi_done, 1)

            def hi_ahead(n, k, n0):
                split_hi(n, (n0 + k) % RAW, (n0 + k) % 2)

            def split_x(i, d):
                act.activation(xs_hi[:, d, :], xt_tile(d), ACT.Copy, scale=gain("norm", i * KT + d)).then_inc(x_hi_done, 1)
                if i * KT + d >= 2:
                    act.wait_ge(acc_done, i * KT + d - 1)
                act.activation(sqb[:, d % 2, :], xt_tile(d), ACT.Square).then_inc(sq_done, 1)

            def norm_std(i):
                act.wait_ge(ssq_done, i + 1)
                act.activation(small[:, 1:1 + TT], ps_misc[:, 0:TT], ACT.Sqrt, bias=small[:, 0:1],
                               scale=1.0 / D).then_inc(std_done, 1)

            def silu(n, tile):
                act.wait_ge(unit_read, n + 1)
                act.activation(t1[:, :], t0[:, :], ACT.Silu).then_inc(silu_done, 1)

            def hidden_hi(n, j):
                act.wait_ge(unit_read, n + 1)
                act.activation(a_hi[:, ds(j * T, T)], t2[:, :], ACT.Copy).then_inc(a_hi_done, 1)

            def pair(n, j, tile, n0, norm=None):
                for m in range(2):
                    hi_ahead(n + (2 * m + 2), 2 * m + 2, n0)
                    if norm is not None and m == 0:
                        norm_std(norm)
                    silu(n + 2 * m, tile + m)
                    hi_ahead(n + (2 * m + 3), 2 * m + 3, n0)
                    hidden_hi(n + (2 * m + 1), j + m)

            def ffn(i):
                n0, tile0 = UNIT_BASE[i], FFN_BASE[i]
                pair(n0, 0, tile0, n0, norm=i)
                n, tile = n0, tile0
                for g, tiles in enumerate(GROUPS):
                    with act.Fori(1 if g == 0 else 0, tiles // 2) as it:
                        pair(it * 4 + n, it * 2, it * 2 + tile, n0)
                    n, tile = n + 2 * tiles, tile + tiles
                    if g < len(GROUPS) - 1:
                        with act.Fori(0, KT // 4) as it:
                            for k in range(4):
                                hi_ahead(it * 4 + (n + k + 2), k + 2, n0)
                    else:
                        for d in range(KT):
                            if n + d + 2 < NUNITS:
                                split_hi(n + d + 2, (n + d + 2) % RAW, (n + d + 2) % 2)
                            if i + 1 < len(PHASES):
                                act.wait_ge(x_added, X_BASE[i + 1] - KT + d + 1)
                                split_x(i + 1, d)
                    n += KT

            def square_q(a, n, m):
                act.wait_ge(unit_read, n + 1)
                if a:
                    act.wait_ge(hssq_done, a)
                act.activation(sqb[:, m, :], (t0, t1)[m][:, :], ACT.Square).then_inc((q_sq_done, k_sq_done)[m], 1)

            def q_high(a):
                if a >= 2:
                    act.wait_ge(score_done, 8 * (a - 1))
                act.activation(q_hi[:, a % 2, :], t0[:, :], ACT.Copy, scale=gq8[:, a // 4:a // 4 + 1]).then_inc(q_hi_done, 1)

            def head_std(a):
                act.wait_ge(hssq_done, a + 1)
                if a:
                    act.wait_ge(hinv_done, a)
                act.activation(hstd[:, :], ps_misc[:, 0:16], ACT.Sqrt, bias=small[:, 0:1], scale=1.0 / HD).then_inc(hstd_done, 1)

            def v_high(a):
                act.wait_ge(vt_done, a + 1)
                if a >= 2:
                    act.wait_ge(pv_done, 2 * (a - 1))
                v = ps_misc[:, :].rearrange("p (t f) -> p t f", f=P)
                for h in range(2):
                    ins = act.activation(v_hi[:, a % 2, :, 2 * h * HD:2 * h * HD + HD], v[:, :, h * HD:(h + 1) * HD], ACT.Copy)
                ins.then_inc(v_hi_done, 1)

            def k_high(a):
                act.wait_ge(kn_done, a + 1)
                if a >= 2:
                    act.wait_ge(score_done, 8 * (a - 1))
                act.activation(k_hi[:, a % 2, :], t1[:, :], ACT.Copy).then_inc(k_hi_done, 1)

            def exp(a, r):
                R, n = 8 * a + r, (r % 4 + 1) * P
                act.wait_ge(negmax_done, R + 1)
                p = probs[:, R % 2, 0:n]
                act.activation(p, p, ACT.Exp, bias=negmax[:, R % 2:R % 2 + 1], accum_out=rowsum[:, R % 2:R % 2 + 1]).then_inc(exp_done, 1)

            def pt_high(a, r):
                R, n = 8 * a + r, r % 4 + 1
                act.wait_ge(turned_done, R + 1)
                act.activation(pt_hi[:, 0:n, (n - 1) * P:n * P],
                               ps_t[:, R % 2, 0:n * P].rearrange("p (j t) -> p j t", t=P), ACT.Copy).then_inc(pt_hi_done, 1)

            def y_high(a):
                act.wait_ge(pv_done, 2 * (a + 1))
                act.activation(a_hi[:, (4 + a % 4) * T:(5 + a % 4) * T], ps_y[:, :], ACT.Copy).then_inc(y_hi_done, 1)

            def attend(a, p, first):
                if p == 0 and not first:
                    y_high(a - 1)
                for r in (2 * p - 2, 2 * p - 1):
                    if r >= 0:
                        pt_high(a, r)
                if p < 4:
                    exp(a, 2 * p)
                    exp(a, 2 * p + 1)

            def pair_in(a, u, n):
                if u == 0:
                    square_q(a, n, 0)
                    q_high(a)
                if u == 1:
                    square_q(a, n, 1)
                if u == 2:
                    head_std(a)
                if u == 3:
                    v_high(a)
                if u == 4:
                    k_high(a)

            def lru(j, u, n):
                if 0 <= j < 4:
                    if u == 1:
                        act.wait_ge(gate_r_done, j + 1)
                        act.activation(ra, ps_y[:, :], ACT.Sigmoid, bias=gain("ra_b", j)).then_inc(sig_r_done, 1)
                    if u == 2:
                        act.wait_ge(gate_i_done, j + 1)
                        act.activation(ri, ps_y[:, :], ACT.Sigmoid, bias=gain("ix_b", j)).then_inc(sig_i_done, 1)
                        act.wait_ge(sig_r_done, j + 1)
                        act.activation(half[:, :], ra, ACT.Tanh, scale=c8[:, j:j + 1]).then_inc(tanh_done, 1)
                        act.wait_ge(tanh_done, j + 1)
                        act.activation(ra, ra, ACT.Exp, scale=c8[:, 4 + j:5 + j]).then_inc(decay_done, 1)
                        act.wait_ge(decay_done, j + 1)
                        act.activation(hh, ra, ACT.Square).then_inc(sqa_done, 1)
                    if u == 3:
                        act.wait_ge(mult2_done, j + 1)
                        act.activation(half[:, :], half[:, :], ACT.Sqrt).then_inc(mult_done, 1)
                    if u == 4:
                        act.wait_ge(ly_done, j + 1)
                        act.activation(a_hi[:, j * T:(j + 1) * T], hh, ACT.Copy).then_inc(l_hi_done, 1)
                if j < 3 and u == 4:
                    act.wait_ge(conv_done, 4 * (j + 2))
                    act.activation(xc_hi[:, :], xc, ACT.Copy).then_inc(xc_hi_done, 1)
                    act.wait_ge(unit_read, n + 1)
                    g = gelu[(j + 1) % 2]
                    act.activation(g, g, ACT.Gelu_apprx_tanh).then_inc(gelu_done, 1)

            def split_bd():
                act.wait_ge(c_landed, 16 * 5)
                act.activation(bdr_hi[:, :, :, :].rearrange("p a b c -> p (a b c)"), bd_raw, ACT.Copy).then_inc(bd_hi_done, 1)

            def out_tail(i, n, a0, lru_too):
                for u in range(5):
                    attend(a0 + 3, u, False)
                    if lru_too:
                        lru(3, u, n)
                y_high(a0 + 3)

            def add_out(i, n):
                for d in range(KT):
                    split_hi(n + d + 2, (n + d + 2) % RAW, (n + d + 2) % 2)
                    act.wait_ge(unit_read, n + d + 1)
                    split_x(i + 1, d)

            def even(i):
                n0 = UNIT_BASE[i]
                act.wait_ge(sp_done, 2)
                act.activation(sp[:, 4:8], sp[:, 0:4], ACT.Exp, scale=-1.0).then_inc(spe_done, 1)
                for it in range(4):
                    for u in range(5):
                        n = n0 + 5 * it + u
                        if it * 5 + u < 1:
                            split_hi(n + 2, (n + 2) % RAW, (n + 2) % 2)
                            norm_std(i)
                        else:
                            split_hi(n + 2, (n + 2) % RAW, (n + 2) % 2)
                        if it:
                            attend(it - 1, u, it == 1)
                        pair_in(it, u, n)
                        lru(it - 1, u, n)
                out_tail(i, n0 + MIX_IN, 0, True)
                add_out(i, n0 + MIX_IN)

            def index_row(q):
                n = (2 + q // HEADS) * P
                act.wait_ge(idx_done, q + 1)
                if q >= 2:
                    act.wait_ge(isc_done, q - 1)
                act.activation(relu[q % 2][:, 0:n], ps_s[:, q % 2, 0:n], ACT.Relu).then_inc(relu_done, 1)

            def odd(i):
                n0 = UNIT_BASE[i]
                for u in range(IDX_IN):
                    n = n0 + u
                    split_hi(n + 2, (n + 2) % RAW, (n + 2) % 2)
                    if u == 0:
                        norm_std(i)
                        act.wait_ge(unit_read, n + 1)
                        act.activation(ki_hi[0:HD, :], t0[0:HD, :], ACT.Copy).then_inc(ki_hi_done, 1)
                        act.wait_ge(ki_lo_done, 1)
                        act.dma_start(ki_hi[HD:P, :].bitcast(F32), ki_hi[0:HD, :].bitcast(F32)).then_inc(ki_landed, 16)
                        act.dma_start(ki_lo[HD:P, :].bitcast(F32), ki_lo[0:HD, :].bitcast(F32)).then_inc(ki_landed, 16)
                    else:
                        act.wait_ge(unit_read, n + 1)
                        act.activation(a_hi[:, (3 + u) * T:(4 + u) * T], t1[:, :], ACT.Copy).then_inc(qi_hi_done, 1)
                for m in range(8):
                    n = n0 + IDX_IN + m
                    split_hi(n + 2, (n + 2) % RAW, (n + 2) % 2)
                    if m % 2:
                        act.wait_ge(unit_read, n + 1)
                        act.activation(t2[:, :], t2[:, :], ACT.Sigmoid).then_inc(glu_sig_done, 1)
                    if m < 4:
                        for q in range(6 * m, 6 * m + 6):
                            index_row(q)
                for it in range(4):
                    for u in range(5):
                        n = n0 + IDX_IN + 8 + 3 * it + u
                        if u < 3:
                            split_hi(n + 2, (n + 2) % RAW, (n + 2) % 2)
                        if it:
                            attend(4 + it - 1, u, it == 1)
                        pair_in(4 + it, u, n)
                out_tail(i, n0 + IDX_IN + MIX_IN, 4, False)
                for c in range(4):
                    act.wait_ge(cen_done, c + 1)
                    act.activation(squares[c], cv[c], ACT.Square).then_inc(cen_sq_done, 1)
                act.wait_ge(var_mm, 1)
                act.activation(hstd[:, 0:TT], ps_misc[:, 0:TT], ACT.Sqrt, bias=small[:, 0:1], scale=1.0 / (4 * P)).then_inc(ln_std_done, 1)
                for c in range(4):
                    act.wait_ge(scaled_done, c + 1)
                    act.activation(cv[c], cv[c], ACT.Silu, bias=gain("ln_b", c)).then_inc(cy_done, 1)
                    act.wait_ge(cy_done, c + 1)
                    act.activation(a_hi[:, c * T:(c + 1) * T], cv[c], ACT.Copy).then_inc(l_hi_done, 1)
                add_out(i, n0 + IDX_IN + MIX_IN)

            act.dma_start(relb, relb_in).then_inc(c_landed, 16)
            act.dma_start(onehot, onehot_in).then_inc(c_landed, 16)
            act.dma_start(vec[:, :], vec_in).then_inc(c_landed, 16)
            for d in range(KT):
                act.dma_start(xt_tile(d), xt_in[d]).then_inc(x_landed, 16)
            act.dma_start(ident[:, :], ident_in).then_inc(c_landed, 16)
            act.dma_start(bd_raw, bd_in).then_inc(c_landed, 16)
            act.wait_ge(x_landed, 16 * KT)
            act.wait_ge(c_landed, 16 * 5)
            act.wait_ge(const_done, 12)
            for d in range(KT):
                if d < 2:
                    split_hi(d, d, d, is_first=True)
                split_x(0, d)
            split_bd()
            act.wait_ge(table_done, 1)
            act.dma_start(skew, table.rearrange("h (o y) -> h o y", o=1).to_broadcast([HEADS, P, SKEW])).then_inc(skewed, 16)
            act.wait_ge(skewed, 16)
            act.dma_start(bias_t[:, :, :], skew.rearrange("h p y -> h (p y)")[:, P - 1:P - 1 + P * (SKEW - 1)].rearrange(
                "h (p y) -> p h y", y=SKEW - 1)[:, :, 0:T]).then_inc(bias_landed, 16)
            for i, phase in enumerate(PHASES):
                {"ffn": ffn, "even": even, "odd": odd}[phase](i)

        @block.vector
        def _(dve):
            def split_lo(n, slot, s):
                dve.wait_ge(w_hi_done, n + 1)
                dve.tensor_tensor(w_lo[:, s, :], raw[:, slot, :], w_hi[:, s, :].bitcast(F32),
                                  ALU.subtract).then_inc(w_lo_done, 1)

            def lo_ahead(n, k, n0):
                split_lo(n, (n0 + k) % RAW, (n0 + k) % 2)

            def split_x(i, d):
                dve.wait_ge(x_hi_done, i * KT + d + 1)
                dve.scalar_tensor_tensor(xs_lo[:, d, :], xt_tile(d), gain("norm", i * KT + d),
                                         xs_hi[:, d, :].bitcast(F32), ALU.mult, ALU.subtract).then_inc(x_lo_done, 1)
                dve.wait_ge(sq_done, i * KT + d + 1)
                if d == 0:
                    if i:
                        dve.wait_ge(ssq_done, i)
                    dve.tensor_copy(acc[:, :], sqb[:, 0, :]).then_inc(acc_done, 1)
                else:
                    dve.wait_ge(acc_done, i * KT + d)
                    dve.tensor_tensor(acc[:, :], acc[:, :], sqb[:, d % 2, :], ALU.add).then_inc(acc_done, 1)

            def norm_diag(i):
                dve.wait_ge(std_done, i + 1)
                dve.reciprocal(rcol[:, :], small[:, 1:1 + TT]).then_inc(rcol_done, 1)
                dve.wait_ge(rcol_done, i + 1)
                for t in range(TT):
                    ins = dve.tensor_scalar(diag[:, t * P:(t + 1) * P], ident[:, :], rcol[:, t:t + 1], None, ALU.mult)
                ins.then_inc(diag_done, 1)

            def norm_rstd(i):
                dve.wait_ge(rbc_done, i + 1)
                dve.tensor_copy(rstd[:, :], ps_misc[:, :]).then_inc(rstd_done, 1)
                dve.wait_ge(rstd_done, i + 1)
                dve.tensor_scalar(half[:, :], rstd[:, :], 0.5, None, ALU.mult).then_inc(half_done, 1)

            def gate(n, s, tile):
                dve.wait_ge(unit_done, n + 1)
                if type(tile) is not int or tile > 0:
                    dve.wait_ge(silu_done, tile)
                dve.tensor_tensor(t0[:, :], ps_unit[:, s, :], rstd[:, :], ALU.mult).then_inc(unit_read, 1)

            def up(n, s, tile):
                dve.wait_ge(unit_done, n + 1)
                dve.wait_ge(silu_done, tile + 1)
                if type(tile) is not int or tile > 0:
                    dve.wait_ge(a_hi_done, tile)
                dve.tensor_tensor(t2[:, :], ps_unit[:, s, :], t1[:, :], ALU.mult).then_inc(unit_read, 1)

            def hidden_lo(j, tile):
                dve.wait_ge(a_hi_done, tile + 1)
                dve.tensor_tensor(a_lo[:, ds(j * T, T)], t2[:, :], a_hi[:, ds(j * T, T)].bitcast(F32),
                                  ALU.subtract).then_inc(a_lo_done, 1)

            def pair(n, j, tile, n0, norm=None):
                for m in range(2):
                    if norm is not None and m == 0:
                        lo_ahead(n + 2, 2, n0)
                        norm_diag(norm)
                        norm_rstd(norm)
                        dve.wait_ge(half_done, norm_count(norm))
                    gate(n + 2 * m, (n0 + 2 * m) % 2, tile + m)
                    if norm is None or m == 1:
                        lo_ahead(n + (2 * m + 2), 2 * m + 2, n0)
                    up(n + (2 * m + 1), (n0 + 2 * m + 1) % 2, tile + m)
                    lo_ahead(n + (2 * m + 3), 2 * m + 3, n0)
                    hidden_lo(j + m, tile + m)

            def norm_count(i):
                return i + 1

            def add_down(n, s, d, x_count):
                dve.wait_ge(unit_done, n + 1)
                if type(x_count) is not int or x_count > 0:
                    dve.wait_ge(x_added, x_count)
                dve.tensor_tensor(t0[:, :], ps_unit[:, s, :], half[:, :], ALU.mult).then_inc(unit_read, 1)
                dve.wait_ge(unit_read, n + 1)
                dve.tensor_tensor(xt_tile(d), xt_tile(d), t0[:, :], ALU.add).then_inc(x_added, 1)

            def ffn(i):
                n0, tile0 = UNIT_BASE[i], FFN_BASE[i]
                pair(n0, 0, tile0, n0, norm=i)
                n, tile = n0, tile0
                for g, tiles in enumerate(GROUPS):
                    with dve.Fori(1 if g == 0 else 0, tiles // 2) as it:
                        pair(it * 4 + n, it * 2, it * 2 + tile, n0)
                    n, tile = n + 2 * tiles, tile + tiles
                    dve.wait_ge(silu_done, tile)
                    if g < len(GROUPS) - 1:
                        with dve.Fori(0, KT // 4) as it:
                            for k in range(4):
                                add_down(it * 4 + (n + k), (n0 + k) % 2, it * 4 + k, it * 4 + (X_BASE[i] + g * KT + k))
                                lo_ahead(it * 4 + (n + k + 2), k + 2, n0)
                        dve.wait_ge(x_added, X_BASE[i] + (g + 1) * KT)
                    else:
                        for d in range(KT):
                            add_down(n + d, (n + d) % 2, d, X_BASE[i] + g * KT + d)
                            if i + 1 < len(PHASES):
                                split_x(i + 1, d)
                            if n + d + 2 < NUNITS:
                                split_lo(n + d + 2, (n + d + 2) % RAW, (n + d + 2) % 2)
                    n += KT

            def q_scaled(a, n):
                dve.wait_ge(unit_done, n + 1)
                if a:
                    dve.wait_ge(q_lo_done, a)
                dve.tensor_tensor(t0[:, :], ps_unit[:, n % 2, :], rstd[:, :], ALU.mult).then_inc(unit_read, 1)

            def q_low(a):
                dve.wait_ge(q_hi_done, a + 1)
                dve.scalar_tensor_tensor(q_lo[:, a % 2, :], t0[:, :], gq8[:, a // 4:a // 4 + 1],
                                         q_hi[:, a % 2, :].bitcast(F32), ALU.mult, ALU.subtract).then_inc(q_lo_done, 1)

            def k_scaled(a, n):
                dve.wait_ge(unit_done, n + 1)
                if a:
                    dve.wait_ge(k_lo_done, a)
                dve.tensor_tensor(t1[:, :], ps_unit[:, n % 2, :], rstd[:, :], ALU.mult).then_inc(unit_read, 1)

            def v_scaled(a, n):
                dve.wait_ge(unit_done, n + 1)
                if a:
                    dve.wait_ge(vt_done, a)
                dve.tensor_tensor(t2[:, :], ps_unit[:, n % 2, :], rstd[:, :], ALU.mult).then_inc(unit_read, 1)

            def head_inv(a):
                dve.wait_ge(hstd_done, a + 1)
                if a >= 2:
                    dve.wait_ge(biased_done, 8 * (a - 1))
                dve.reciprocal(hinv[:, a % 2, :], hstd[:, :]).then_inc(hinv_done, 1)
                dve.wait_ge(hinv_done, a + 1)
                if a:
                    dve.wait_ge(kbc_done, a)
                for h in range(2):
                    for t in range(TT):
                        c = (TT + t) * 2 + h
                        ins = dve.tensor_scalar((diag, acc)[h][:, t * P:(t + 1) * P], ident[:, :], hinv[:, a % 2, c:c + 1], None, ALU.mult)
                ins.then_inc(kdiag_done, 1)

            def k_normed(a):
                dve.wait_ge(kbc_done, a + 1)
                dve.scalar_tensor_tensor(t1[:, :], t1[:, :], gain("ev_k" if a < 4 else "od_k", 0), ps_misc[:, :],
                                         ALU.mult, ALU.mult).then_inc(kn_done, 1)

            def k_low(a):
                dve.wait_ge(k_hi_done, a + 1)
                dve.tensor_tensor(k_lo[:, a % 2, :], t1[:, :], k_hi[:, a % 2, :].bitcast(F32), ALU.subtract).then_inc(k_lo_done, 1)

            def v_low(a):
                dve.wait_ge(v_hi_done, a + 1)
                v = ps_misc[:, :].rearrange("p (t f) -> p t f", f=P)
                for h in range(2):
                    w = slice(2 * h * HD, 2 * h * HD + HD)
                    ins = dve.tensor_tensor(v_lo[:, a % 2, :, w], v[:, :, h * HD:(h + 1) * HD],
                                            v_hi[:, a % 2, :, w].bitcast(F32), ALU.subtract)
                ins.then_inc(v_lo_done, 1)

            def row_bias(a, r):
                R, h, t = 8 * a + r, r // 4, r % 4
                n = (t + 1) * P
                p = probs[:, R % 2, 0:n]
                dve.wait_ge(score_done, R + 1)
                if R >= 2:
                    dve.wait_ge(turned_done, R - 1)
                if R == 0:
                    dve.wait_ge(bias_landed, 16)
                c = 2 * t + h
                dve.scalar_tensor_tensor(p, ps_s[:, R % 2, 0:n], hinv[:, a % 2, c:c + 1],
                                         bias_t[:, 2 * (a % 4) + h, T - n:T], ALU.mult, ALU.add).then_inc(biased_done, 1)
                dve.wait_ge(biased_done, R + 1)
                if a >= 4 and t:
                    dve.tensor_tensor(p, p, keep(t), ALU.add).then_inc(masked_done, 1)
                    dve.wait_ge(masked_done, 3 * (2 * (a - 4) + h) + t)
                if R >= 2:
                    dve.wait_ge(negmax_done, R - 1)
                dve.reduce_max(rowmax[:, R % 2:R % 2 + 1], p, AX_X).then_inc(rowmax_done, 1)
                dve.wait_ge(rowmax_done, R + 1)
                if R >= 2:
                    dve.wait_ge(exp_done, R - 1)
                dve.tensor_scalar(negmax[:, R % 2:R % 2 + 1], rowmax[:, R % 2:R % 2 + 1], -1.0, None, ALU.mult).then_inc(negmax_done, 1)

            def row_norm(a, r):
                R, n = 8 * a + r, (r % 4 + 1) * P
                p, inv = probs[:, R % 2, 0:n], rowinv[:, R % 2:R % 2 + 1]
                dve.wait_ge(exp_done, R + 1)
                if R >= 2:
                    dve.wait_ge(prob_done, R - 1)
                dve.reciprocal(inv, rowsum[:, R % 2:R % 2 + 1]).then_inc(rowinv_done, 1)
                dve.wait_ge(rowinv_done, R + 1)
                dve.tensor_scalar(p, p, inv, None, ALU.mult).then_inc(prob_done, 1)

            def pt_low(a, r):
                R, n = 8 * a + r, r % 4 + 1
                w = slice((n - 1) * P, n * P)
                dve.wait_ge(pt_hi_done, R + 1)
                dve.tensor_tensor(pt_lo[:, 0:n, w], ps_t[:, R % 2, 0:n * P].rearrange("p (j t) -> p j t", t=P),
                                  pt_hi[:, 0:n, w].bitcast(F32), ALU.subtract).then_inc(pt_lo_done, 1)

            def y_low(a):
                dve.wait_ge(y_hi_done, a + 1)
                w = slice((4 + a % 4) * T, (5 + a % 4) * T)
                dve.tensor_tensor(a_lo[:, w], ps_y[:, :], a_hi[:, w].bitcast(F32), ALU.subtract).then_inc(y_lo_done, 1)

            def attend(a, p, first):
                if p == 0 and not first:
                    y_low(a - 1)
                for r in (2 * p - 2, 2 * p - 1):
                    if r >= 0:
                        pt_low(a, r)
                if p < 4:
                    row_bias(a, 2 * p)
                    row_bias(a, 2 * p + 1)

            def attend_end(a, p):
                if p < 4:
                    row_norm(a, 2 * p)
                    row_norm(a, 2 * p + 1)

            def pair_read(a, u, n):
                if u < 3:
                    (q_scaled, k_scaled, v_scaled)[u](a, n)

            def pair_in(a, u):
                if u == 0:
                    q_low(a)
                if u == 2:
                    head_inv(a)
                if u == 3:
                    v_low(a)
                if u == 4:
                    k_normed(a)
                    k_low(a)

            def lru_in(j, n):
                dve.wait_ge(unit_done, n + 1)
                dve.wait_ge(pad_done, 1)
                if j:
                    dve.wait_ge(conv_done, 4 * j)
                dve.tensor_tensor(xr_pad[:, TAPS - 1:TAPS - 1 + T], ps_unit[:, n % 2, :], rstd[:, :], ALU.mult).then_inc(unit_read, 1)

            def lru_conv(j, n):
                dve.wait_ge(unit_read, n + 1)
                if j:
                    dve.wait_ge(ix_done, j)
                for k in range(TAPS):
                    src, w = xr_pad[:, k:k + T], gain("conv_w", TAPS * j + k)
                    if k == 0:
                        dve.tensor_scalar(xc, src, w, gain("conv_b", j), ALU.mult, ALU.add).then_inc(conv_done, 1)
                    else:
                        dve.scalar_tensor_tensor(xc, src, w, xc, ALU.mult, ALU.add).then_inc(conv_done, 1)
                    dve.wait_ge(conv_done, 4 * j + k + 1)

            def gate_in(j, n):
                dve.wait_ge(unit_done, n + 1)
                if j >= 2:
                    dve.wait_ge(ly_done, j - 1)
                dve.tensor_tensor(gelu[j % 2], ps_unit[:, n % 2, :], rstd[:, :], ALU.mult).then_inc(unit_read, 1)

            def lru(j, u, n):
                if 0 <= j < 4:
                    if u == 3:
                        dve.wait_ge(sig_i_done, j + 1)
                        dve.tensor_tensor(ri, ri, xc, ALU.mult).then_inc(ix_done, 1)
                        dve.wait_ge(sqa_done, j + 1)
                        dve.scalar_tensor_tensor(half[:, :], hh, 1.0, half[:, :], ALU.add, ALU.mult).then_inc(mult2_done, 1)
                    if u == 4:
                        dve.wait_ge(mult_done, j + 1)
                        dve.wait_ge(ix_done, j + 1)
                        dve.tensor_tensor(ri, ri, half[:, :], ALU.mult).then_inc(u_done, 1)
                        dve.wait_ge(u_done, j + 1)
                        dve.wait_ge(mult2_done, j + 1)
                        dve.tensor_tensor_scan(hh, ra, ri, 0.0, ALU.mult, ALU.add).then_inc(scan_done, 1)
                        dve.wait_ge(scan_done, j + 1)
                        dve.wait_ge(gelu_done, j + 1)
                        dve.tensor_tensor(hh, hh, gelu[j % 2], ALU.mult).then_inc(ly_done, 1)
                        dve.wait_ge(l_hi_done, j + 1)
                        dve.tensor_tensor(a_lo[:, j * T:(j + 1) * T], hh, a_hi[:, j * T:(j + 1) * T].bitcast(F32), ALU.subtract).then_inc(l_lo_done, 1)
                if j < 3:
                    if u == 3:
                        lru_conv(j + 1, n)
                    if u == 4:
                        dve.wait_ge(xc_hi_done, j + 2)
                        dve.tensor_tensor(xc_lo[:, :], xc, xc_hi[:, :].bitcast(F32), ALU.subtract).then_inc(xc_lo_done, 1)

            def split_bd():
                dve.wait_ge(bd_hi_done, 1)
                dve.tensor_tensor(bdr_lo[:, :, :, :].rearrange("p a b c -> p (a b c)"), bd_raw,
                                  bdr_hi[:, :, :, :].rearrange("p a b c -> p (a b c)").bitcast(F32), ALU.subtract).then_inc(bd_lo_done, 1)

            sp_count = [0]

            def sp_step(ins):
                sp_count[0] += 1
                ins.then_inc(sp_done, 1)
                dve.wait_ge(sp_done, sp_count[0])

            def softplus():
                lam = vec[:, COL["lam"]:COL["lam"] + 4]
                e, z, z2, p = sp[:, 4:8], sp[:, 8:12], sp[:, 12:16], sp[:, 0:4]
                sp_step(dve.tensor_scalar(sp[:, 8:12], lam, -1.0, None, ALU.mult))
                sp_step(dve.tensor_tensor(sp[:, 0:4], lam, sp[:, 8:12], ALU.max))
                dve.wait_ge(spe_done, 1)
                sp_step(dve.tensor_scalar(z2, e, 2.0, None, ALU.add))
                sp_step(dve.reciprocal(z, z2))
                sp_step(dve.tensor_tensor(z, z, e, ALU.mult))
                sp_step(dve.tensor_tensor(z2, z, z, ALU.mult))
                sp_step(dve.tensor_scalar(p, z2, 1.0 / 17, 1.0 / 15, ALU.mult, ALU.add))
                for c in (13, 11, 9, 7, 5, 3, 1):
                    sp_step(dve.tensor_tensor(p, p, z2, ALU.mult))
                    sp_step(dve.tensor_scalar(p, p, 1.0 / c, None, ALU.add))
                sp_step(dve.tensor_tensor(p, p, z, ALU.mult))
                sp_step(dve.tensor_scalar(z2, lam, -1.0, 0.0, ALU.mult, ALU.max))
                sp_step(dve.scalar_tensor_tensor(p, p, 2.0, z2, ALU.mult, ALU.add))
                sp_step(dve.tensor_scalar(c8[:, 0:4], p, LRU_C, None, ALU.mult))
                sp_step(dve.tensor_scalar(c8[:, 4:8], p, -LRU_C, None, ALU.mult))

            def add_out(i, n):
                for d in range(KT):
                    dve.wait_ge(unit_done, n + d + 1)
                    dve.tensor_tensor(xt_tile(d), xt_tile(d), ps_unit[:, (n + d) % 2, :], ALU.add).then_inc(unit_read, 1)
                    dve.wait_ge(unit_read, n + d + 1)
                    split_x(i + 1, d)
                    split_lo(n + d + 2, (n + d + 2) % RAW, (n + d + 2) % 2)

            def even(i):
                n0 = UNIT_BASE[i]
                dve.memset(xr_pad[:, 0:TAPS - 1], 0.0).then_inc(pad_done, 1)
                softplus()
                for it in range(4):
                    for u in range(5):
                        n = n0 + 5 * it + u
                        if it == 0 and u == 0:
                            split_lo(n + 2, (n + 2) % RAW, (n + 2) % 2)
                            norm_diag(i)
                            norm_rstd(i)
                            dve.wait_ge(half_done, i + 1)
                        pair_read(it, u, n)
                        if u == 3:
                            lru_in(it, n)
                        if u == 4:
                            gate_in(it, n)
                        if it or u:
                            split_lo(n + 2, (n + 2) % RAW, (n + 2) % 2)
                        if it:
                            attend(it - 1, u, it == 1)
                        pair_in(it, u)
                        if it:
                            attend_end(it - 1, u)
                        lru(it - 1, u, n)
                for u in range(5):
                    attend(3, u, False)
                    attend_end(3, u)
                    lru(3, u, None)
                y_low(3)
                add_out(i, n0 + MIX_IN)

            def keep(t):
                start = (2, 5, 9)[t - 1] - (t + 1)
                return isc[:, start * P:(start + t + 1) * P]

            def index_row(q):
                t, h = 1 + q // HEADS, q % HEADS
                w = wi[:, t * HEADS + h:t * HEADS + h + 1]
                dve.wait_ge(relu_done, q + 1)
                r = relu[q % 2][:, 0:(t + 1) * P]
                if h == 0:
                    dve.tensor_scalar(keep(t), r, w, None, ALU.mult).then_inc(isc_done, 1)
                else:
                    dve.wait_ge(isc_done, q)
                    dve.scalar_tensor_tensor(keep(t), r, w, keep(t), ALU.mult, ALU.add).then_inc(isc_done, 1)

            cuts = [0]

            def cut_round(c):
                t, r = 1 + c // 16, c % 16
                if r == 0:
                    dve.wait_ge(isc_done, HEADS * t)
                    dve.wait_ge(causal_done, 2)
                    diag_part = keep(t)[:, t * P:(t + 1) * P]
                    dve.tensor_tensor(diag_part, diag_part, causal, ALU.add).then_inc(sel_done, 1)
                    dve.wait_ge(sel_done, 2 * t - 1)
                dve.max(top8, keep(t)).then_inc(top_done, 1)
                dve.wait_ge(top_done, c + 1)
                dve.match_replace(keep(t), top8, keep(t), -3e38).then_inc(cut_done, 1)
                dve.wait_ge(cut_done, c + 1)
                if r == 15:
                    dve.tensor_scalar(keep(t), keep(t), -2e38, NEG, ALU.is_gt, ALU.mult).then_inc(sel_done, 1)
                    dve.wait_ge(sel_done, 2 * t)

            def tap(c):
                j, k = c // DW_TAPS, c % DW_TAPS
                src, w = c_pad[j][:, k:k + T], gain("dw_w", c)
                if k == 0:
                    dve.wait_ge(glu_done, j + 1)
                    dve.tensor_scalar(cv[j], src, w, gain("dw_b", j), ALU.mult, ALU.add).then_inc(dw_done, 1)
                else:
                    dve.wait_ge(dw_done, c)
                    dve.scalar_tensor_tensor(cv[j], src, w, cv[j], ALU.mult, ALU.add).then_inc(dw_done, 1)

            def taps_of(m):
                for c in range(4 * DW_TAPS * m // 20, 4 * DW_TAPS * (m + 1) // 20):
                    tap(c)

            def conv_norm():
                dve.wait_ge(dw_done, 4 * DW_TAPS)
                dve.wait_ge(kbc_done, 8)
                steps = [0]

                def step(ins):
                    steps[0] += 1
                    ins.then_inc(ln_chain, 1)
                    dve.wait_ge(ln_chain, steps[0])
                step(dve.tensor_tensor(acc[:, :], cv[0], cv[1], ALU.add))
                step(dve.tensor_tensor(acc[:, :], acc[:, :], cv[2], ALU.add))
                dve.tensor_tensor(acc[:, :], acc[:, :], cv[3], ALU.add).then_inc(ln_add_done, 1)
                dve.wait_ge(mean_mm, 1)
                for c in range(4):
                    dve.scalar_tensor_tensor(cv[c], ps_misc[:, :], -1.0 / (4 * P), cv[c], ALU.mult, ALU.add).then_inc(cen_done, 1)
                dve.wait_ge(cen_sq_done, 4)
                step(dve.tensor_tensor(acc[:, :], squares[0], squares[1], ALU.add))
                step(dve.tensor_tensor(acc[:, :], acc[:, :], squares[2], ALU.add))
                dve.tensor_tensor(acc[:, :], acc[:, :], squares[3], ALU.add).then_inc(ln_add_done, 1)
                dve.wait_ge(ln_std_done, 1)
                dve.reciprocal(rcol[:, :], hstd[:, 0:TT]).then_inc(ln_rcol_done, 1)
                dve.wait_ge(ln_rcol_done, 1)
                for t in range(TT):
                    ins = dve.tensor_scalar(diag[:, t * P:(t + 1) * P], ident[:, :], rcol[:, t:t + 1], None, ALU.mult)
                ins.then_inc(ln_diag_done, 1)
                dve.wait_ge(ln_bc_done, 1)
                for c in range(4):
                    dve.wait_ge(cen_done, 4)
                    dve.scalar_tensor_tensor(cv[c], cv[c], gain("ln_g", c), ps_misc[:, :], ALU.mult, ALU.mult).then_inc(scaled_done, 1)
                for c in range(4):
                    w = slice(c * T, (c + 1) * T)
                    dve.wait_ge(l_hi_done, 4 + c + 1)
                    dve.tensor_tensor(a_lo[:, w], cv[c], a_hi[:, w].bitcast(F32), ALU.subtract).then_inc(l_lo_done, 1)

            def odd(i):
                n0 = UNIT_BASE[i]
                for j in range(4):
                    dve.memset(c_pad[j][:, 0:DW_TAPS - 1], 0.0).then_inc(pad_done, 1)
                for u in range(IDX_IN):
                    n = n0 + u
                    if u == 0:
                        split_lo(n + 2, (n + 2) % RAW, (n + 2) % 2)
                        norm_diag(i)
                        norm_rstd(i)
                        dve.wait_ge(half_done, i + 1)
                    dve.wait_ge(unit_done, n + 1)
                    if u >= 2:
                        dve.wait_ge(qi_lo_done, u - 1)
                    dve.tensor_tensor((t1 if u else t0)[:, :], ps_unit[:, n % 2, :], rstd[:, :], ALU.mult).then_inc(unit_read, 1)
                    if u:
                        split_lo(n + 2, (n + 2) % RAW, (n + 2) % 2)
                        w = slice((3 + u) * T, (4 + u) * T)
                        dve.wait_ge(qi_hi_done, u)
                        dve.tensor_tensor(a_lo[:, w], t1[:, :], a_hi[:, w].bitcast(F32), ALU.subtract).then_inc(qi_lo_done, 1)
                    else:
                        dve.wait_ge(ki_hi_done, 1)
                        dve.tensor_tensor(ki_lo[0:HD, :], t0[0:HD, :], ki_hi[0:HD, :].bitcast(F32), ALU.subtract).then_inc(ki_lo_done, 1)
                for m in range(8):
                    n = n0 + IDX_IN + m
                    dve.wait_ge(unit_done, n + 1)
                    if m == 0:
                        dve.wait_ge(qi_lo_done, 4)
                    elif m >= 2:
                        dve.wait_ge(glu_done, m // 2)
                    dve.tensor_tensor((t1, t2)[m % 2][:, :], ps_unit[:, n % 2, :], rstd[:, :], ALU.mult).then_inc(unit_read, 1)
                    split_lo(n + 2, (n + 2) % RAW, (n + 2) % 2)
                    if m == 0:
                        dve.wait_ge(wi_turned, 1)
                        w = ps_misc[:, :].rearrange("p (t f) -> p t f", f=P)[:, :, HD:HD + HEADS]
                        dve.tensor_scalar(wi.rearrange("p (t h) -> p t h", h=HEADS), w, (HD ** -0.5) * (HEADS ** -0.5), None,
                                          ALU.mult).then_inc(wi_done, 1)
                        dve.wait_ge(wi_done, 1)
                    if m < 4:
                        for q in range(6 * m, 6 * m + 6):
                            index_row(q)
                    if m % 2:
                        dve.wait_ge(glu_sig_done, m // 2 + 1)
                        dve.tensor_tensor(c_pad[m // 2][:, DW_TAPS - 1:], t1[:, :], t2[:, :], ALU.mult).then_inc(glu_done, 1)
                    if m:
                        for c in range(5 * m - 5, 5 * m):
                            cut_round(c)
                for it in range(4):
                    for u in range(5):
                        n = n0 + IDX_IN + 8 + 3 * it + u
                        if u < 3:
                            if it == 0 and u == 0:
                                dve.wait_ge(glu_done, 4)
                            pair_read(4 + it, u, n)
                            split_lo(n + 2, (n + 2) % RAW, (n + 2) % 2)
                        if it == 0:
                            for c in range(35 + 5 * u, min(40 + 5 * u, 48)):
                                cut_round(c)
                        if it:
                            attend(4 + it - 1, u, it == 1)
                        pair_in(4 + it, u)
                        if it:
                            attend_end(4 + it - 1, u)
                        taps_of(5 * it + u)
                for u in range(5):
                    attend(7, u, False)
                    attend_end(7, u)
                y_low(7)
                conv_norm()
                add_out(i, n0 + IDX_IN + MIX_IN)

            dve.wait_ge(const_done, 12)
            dve.wait_ge(c_landed, 16 * 5)
            for c, name in enumerate(("ev_q", "od_q")):
                dve.tensor_scalar(gq8[:, c:c + 1], gain(name, 0), HD ** -0.5, None, ALU.mult).then_inc(gq_done, 1)
            for d in range(KT):
                if d < 2:
                    split_lo(d, d, d)
                split_x(0, d)
            split_bd()
            dve.wait_ge(table_mm, 1)
            dve.tensor_copy(table[:, 0:T], ps_y[0:HEADS, :]).then_inc(table_done, 1)
            for i, phase in enumerate(PHASES):
                {"ffn": ffn, "even": even, "odd": odd}[phase](i)


def columns(w, start, tiles):
    part = w[:, start:start + tiles * P]
    return part.reshape(KT, P, tiles, P).transpose(2, 1, 0, 3).reshape(tiles, P, UNIT)


def ffn_units(w_gate, w_up, w_down):
    gate_up = np.stack([columns(w_gate, 0, FT), columns(w_up, 0, FT)], 1).reshape(2 * FT, P, UNIT)
    down = w_down.reshape(FT, P, KT, P).transpose(2, 1, 0, 3)
    parts, f = [], 0
    for tiles in GROUPS:
        parts.append(gate_up[2 * f:2 * (f + tiles)])
        group = np.zeros((KT, P, UNIT), np.float32)
        group[:, :, :tiles * P] = down[:, :, f:f + tiles].reshape(KT, P, tiles * P)
        parts.append(group)
        f += tiles
    return parts


def by_tile(v):
    return v.reshape(-1, P).T


def lay_out(a):
    even, odd = a["ev_w_in"][0], a["od_w_in"][0]
    pair = lambda w, starts, i: [columns(w, s + i * P, 1) for s in starts]
    units = []
    units += ffn_units(a["ffn1_w_gate"][0], a["ffn1_w_up"][0], a["ffn1_w_down"][0])
    for i in range(4):
        units += pair(even, (1024, 1536, 2048, 512, 0), i)
    units.append(columns(a["ev_w_out"][0], 0, KT))
    units += ffn_units(a["ffn2_w_gate"][0], a["ffn2_w_up"][0], a["ffn2_w_down"][0])
    units += ffn_units(a["ffn1_w_gate"][1], a["ffn1_w_up"][1], a["ffn1_w_down"][1])
    kiwi = np.zeros((D, P), np.float32)
    kiwi[:, :HD + HEADS] = odd[:, 3072:3072 + HD + HEADS]
    units.append(columns(kiwi, 0, 1))
    units.append(columns(odd, 2560, 4))
    for i in range(4):
        units += pair(odd, (0, 512), i)
    for i in range(4):
        units += pair(odd, (1024, 1536, 2048), i)
    units.append(columns(a["od_w_out"][0], 0, KT))
    units += ffn_units(a["ffn2_w_gate"][1], a["ffn2_w_up"][1], a["ffn2_w_down"][1])
    w_stream = np.concatenate(units, 0)

    norms = [a["ffn1_norm"][0], a["mix_norm"][0], a["ffn2_norm"][0], a["ffn1_norm"][1], a["mix_norm"][1], a["ffn2_norm"][1]]
    twice = lambda v: np.concatenate([v, v])
    taps = lambda w: w.reshape(w.shape[0], 4, P).transpose(2, 1, 0).reshape(P, -1)
    vec = np.concatenate(
        [by_tile(v) for v in norms]
        + [taps(a["ev_conv_w"][0])] + [by_tile(a[n][0]) for n in ("ev_conv_b", "ev_ra_b", "ev_ix_b", "ev_lambda")]
        + [by_tile(twice(a["ev_q_norm"][0])), by_tile(twice(a["ev_k_norm"][0]))]
        + [taps(a["od_dw_w"][0])] + [by_tile(a[n][0]) for n in ("od_dw_b", "od_ln_g", "od_ln_b")]
        + [by_tile(twice(a["od_q_norm"][0])), by_tile(twice(a["od_k_norm"][0]))], 1)

    bd = np.zeros((P, 2, 4, P), np.float32)
    for g, name in enumerate(("ev_ra_w", "ev_ix_w")):
        for b in range(8):
            at = slice(b % 2 * 64, b % 2 * 64 + 64)
            bd[at, g, b // 2, at] = a[name][0, b]

    distance = np.arange(T - 1, -1, -1)
    large = 16 + (np.log(np.maximum(distance, 1) / 16) / np.log(128 / 16) * 16).astype(np.int64)
    bucket = np.where(distance < 16, distance, np.minimum(large, BUCKETS - 1))
    onehot = (np.arange(BUCKETS)[:, None] == bucket[None, :]).astype(np.float32)

    return {
        "xt_in": a["x"][0].T.reshape(KT, P, T),
        "w_stream": w_stream,
        "vec_in": vec,
        "bd_in": bd.reshape(P, UNIT),
        "relb_in": a["rel_bias"],
        "onehot_in": onehot,
        "ident_in": np.eye(P, dtype=np.float32),
    }


def kernel(**inputs):
    import concourse.bacc as bacc
    from concourse.bass_utils import run_bass_kernel_spmd

    arrays = {k: np.ascontiguousarray(v) for k, v in lay_out({k: np.asarray(v) for k, v in inputs.items()}).items()}
    nc = bacc.Bacc("TRN2", target_bir_lowering=False, num_devices=1, dynamic_dma_scratch_size=1024)
    args = [nc.dram_tensor(k + "_dram", v.shape, mybir.dt.from_np(v.dtype), kind="ExternalInput").ap() for k, v in arrays.items()]
    out = nc.dram_tensor("out_dram", (KT, P, T), F32, kind="ExternalOutput").ap()
    build(nc, *args, out)
    r = run_bass_kernel_spmd(nc, [{k + "_dram": v for k, v in arrays.items()}], core_ids=[0])
    return r.results[0]["out_dram"].reshape(D, T).T[None]
```

```python
from contextlib import ExitStack

import numpy as np

import concourse.bass as bass
from concourse import mybir

F32 = mybir.dt.float32
F32R = mybir.dt.float32r
ALU = mybir.AluOpType
ACT = mybir.ActivationFunctionType
AX_X = mybir.AxisListType.X
ds = bass.ds

P = 128
T = 512
TT = T // P
D = 1024
KT = D // P
DFF = 2816
FT = DFF // P
GROUPS = (8, 8, 6)
UNIT = KT * P
RAW = 4
EPS = 1e-6
NEG = -1e30
HEADS = 8
HD = 64
BUCKETS = 32
TAPS = 4
DW_TAPS = 31
TE_TAPS = 16
VE_TAPS = DW_TAPS - TE_TAPS
LRU_C = 8.0
SKEW = 640

FFN_UNITS = 2 * FT + len(GROUPS) * KT
EVEN_IN = 5
IDX_IN = 5
GLU_IN = 8
EARLY = {"even": (4, 5, 0, 1, 2, 6), "odd": (4, 5, 0, 1, 2, 3, 6)}
READY = {"even": 5, "odd": 2}
LATE = {"even": (3, 7), "odd": (7,)}
SPLIT_TILES = 4
X_AFTER = ((0, 1), (2, 3), (4, 5), (6,), (7,))
OUT_UNITS = KT + 1
CONV_UNITS = TE_TAPS // KT
ODD_IN = [3, 3 + CONV_UNITS, 3 + CONV_UNITS, 3]
EVEN_UNITS = 4 * EVEN_IN + OUT_UNITS
ODD_FIRST = IDX_IN + GLU_IN + 2 * CONV_UNITS
ODD_BASE = [ODD_FIRST + sum(ODD_IN[:i]) for i in range(5)]
ODD_UNITS = ODD_BASE[4] + OUT_UNITS
PHASES = ("ffn", "even", "ffn", "ffn", "odd", "ffn")
PHASE_UNITS = {"ffn": FFN_UNITS, "even": EVEN_UNITS, "odd": ODD_UNITS}
UNIT_BASE = [sum(PHASE_UNITS[p] for p in PHASES[:i]) for i in range(len(PHASES) + 1)]
NUNITS = UNIT_BASE[-1]
X_UPDATES = {"ffn": len(GROUPS) * KT, "even": 0, "odd": 0}
X_BASE = [sum(X_UPDATES[p] for p in PHASES[:i]) for i in range(len(PHASES) + 1)]
LATE_BASE = [sum(SPLIT_TILES - 1 for p in PHASES[:i] if p in LATE) for i in range(len(PHASES) + 1)]
FFN_BASE = [FT * PHASES[:i].count("ffn") for i in range(len(PHASES) + 1)]

VEC_SIZES = (("norm", len(PHASES) * KT), ("conv_w", 4 * TAPS), ("conv_b", 4), ("ra_b", 4), ("ix_b", 4),
             ("lam", 4), ("ev_q", 1), ("ev_k", 1), ("dw_w", 4 * DW_TAPS), ("dw_b", 4), ("ln_g", 4),
             ("ln_b", 4), ("od_q", 1), ("od_k", 1))
COL = {}
NVEC = 0
for _name, _n in VEC_SIZES:
    COL[_name] = NVEC
    NVEC += _n


def build(nc, xt_in, w_stream, vec_in, bd_in, relb_in, onehot_in, ident_in, out):
    with ExitStack() as ctx:
        top = [(nc.sbuf_base + 31) // 32 * 32]

        def sb(name, shape, dt=F32, at=None):
            size = int(np.prod(shape[1:])) * 4
            if at is None:
                at, top[0] = top[0], top[0] + (size + 31) // 32 * 32
            return nc.alloc_sbuf_tensor_at(name, shape, dt, offset=at)

        def sem(name):
            return ctx.enter_context(nc.semaphore(name))

        xt = sb("xt", [P, KT * T])
        xs_hi = sb("xs_hi", [P, KT, T], F32R)
        xs_lo = sb("xs_lo", [P, KT, T], F32R)
        raw = sb("raw", [P, RAW, UNIT])
        w_hi = sb("w_hi", [P, 2, UNIT], F32R)
        w_lo = sb("w_lo", [P, 2, UNIT], F32R)
        a_hi = sb("a_hi", [P, 8 * T], F32R)
        gelu_1_at = top[0] + 7 * T * 4
        a_lo = sb("a_lo", [P, 8 * T], F32R)
        vec = sb("vec", [P, NVEC])
        ident = sb("ident", [P, P])
        ones = sb("ones", [P, P])
        small = sb("small", [P, 8])
        rcol = sb("rcol", [P, TT])
        rstd = sb("rstd", [P, T])
        half = sb("half", [P, T])
        t0 = sb("t0", [P, T])
        t1 = sb("t1", [P, T])
        t2 = sb("t2", [P, T])
        sqb = sb("sqb", [P, 2, T])
        acc = sb("acc", [P, T])
        diag = sb("diag", [P, T])

        bias_t = sb("bias_t", [P, HEADS, T])
        c8 = sb("c8", [P, 8])[:, :]
        sp = sb("sp", [P, 16])[:, :]
        gq8 = sb("gq8", [P, 2])
        head_sel = sb("head_sel", [P, 2])
        head_row = sb("head_row", [P, 3 * HD])
        q_hi = sb("q_hi", [P, 2, T], F32R)
        q_lo = sb("q_lo", [P, 2, T], F32R)
        k_hi = sb("k_hi", [P, 2, T], F32R)
        k_lo = sb("k_lo", [P, 2, T], F32R)
        v_hi = sb("v_hi", [P, 2, TT, 3 * HD], F32R)
        v_lo = sb("v_lo", [P, 2, TT, 3 * HD], F32R)
        hstd = sb("hstd", [P, 16])
        hinv = sb("hinv", [P, 2, 16])
        probs = sb("probs", [P, 2, T])
        negmax = sb("negmax", [P, 2])
        rowsum = sb("rowsum", [P, 2])
        rowinv = sb("rowinv", [P, 2])
        pt_hi = sb("pt_hi", [P, TT, T], F32R)
        pt_lo = sb("pt_lo", [P, TT, T], F32R)
        shared = top[0]
        bdr_hi = sb("bdr_hi", [P, 2, 4, P], F32R)
        bdr_lo = sb("bdr_lo", [P, 2, 4, P], F32R)
        xc_hi = sb("xc_hi", [P, T], F32R)
        xc_lo = sb("xc_lo", [P, T], F32R)
        xr_pad = sb("xr_pad", [P, T + TAPS])[:, :]
        xc = sb("xc", [P, T])[:, :]
        gelu = [sb("gelu_0", [P, T])[:, :], sb("gelu_1", [P, T], at=gelu_1_at)[:, :]]
        ra = sb("ra", [P, T])[:, :]
        ri = sb("ri", [P, T])[:, :]
        hh = sb("hh", [P, T])[:, :]
        even_top = top[0]
        top[0] = shared
        causal = sb("causal", [P, P])[:, :]
        isc = sb("isc", [P, P * (2 + 3 + 4)])[:, :]
        top8 = sb("top8", [P, 8])[:, :]
        wi = sb("wi", [P, TT * HEADS])[:, :]
        relu = [probs[:, 0, :], probs[:, 1, :]]
        c_pad = [sb(f"c_pad{j}", [P, T + DW_TAPS - 1])[:, :] for j in range(4)]
        cv = [sb(f"cv{j}", [P, T])[:, :] for j in range(4)]
        ki_hi = sb("ki_hi", [P, T], F32R)
        ki_lo = sb("ki_lo", [P, T], F32R)
        branch_sum = c_pad[0][:, 0:T]
        branch_inv = c_pad[1][:, 0:T]
        branch_diag = c_pad[2][:, 0:T]
        squares = [c[:, 0:T] for c in c_pad]
        odd_top = top[0]
        top[0] = shared + 2 * 4 * UNIT
        table = sb("table", [HEADS, SKEW])[:, :]
        relb = sb("relb", [BUCKETS, HEADS])[:, :]
        onehot = sb("onehot", [BUCKETS, T])[:, :]
        bd_raw = sb("bd_raw", [P, UNIT])[:, :]
        assert max(even_top, odd_top, top[0]) <= nc.sbuf_usable_end, (even_top, odd_top)
        skew = nc.dram_tensor("skew", [HEADS, P, SKEW], F32).ap()

        ps_s = ctx.enter_context(nc.psum_tensor("ps_s", [P, 2, T], F32))
        ps_t = ctx.enter_context(nc.psum_tensor("ps_t", [P, 2, T], F32))
        ps_unit = ctx.enter_context(nc.psum_tensor("ps_unit", [P, 2, T], F32))
        ps_misc = ctx.enter_context(nc.psum_tensor("ps_misc", [P, T], F32))
        ps_y = ctx.enter_context(nc.psum_tensor("ps_y", [P, T], F32))

        w_landed = [sem(f"w_landed{s}") for s in range(RAW)]
        w_hi_done = sem("w_hi_done")
        w_lo_done = sem("w_lo_done")
        unit_done = sem("unit_done")
        late_done = sem("late_done")
        late_read = sem("late_read")
        unit_read = sem("unit_read")
        silu_done = sem("silu_done")
        a_hi_done = sem("a_hi_done")
        a_lo_done = sem("a_lo_done")
        x_landed = [sem(f"x_landed{d}") for d in range(KT)]
        vec_landed = sem("vec_landed")
        c_landed = sem("c_landed")
        x_added = sem("x_added")
        x_hi_done = sem("x_hi_done")
        x_lo_done = sem("x_lo_done")
        sq_done = sem("sq_done")
        acc_done = sem("acc_done")
        ssq_done = sem("ssq_done")
        std_done = sem("std_done")
        rcol_done = sem("rcol_done")
        diag_done = sem("diag_done")
        rbc_done = sem("rbc_done")
        rstd_done = sem("rstd_done")
        half_done = sem("half_done")
        const_done = sem("const_done")
        q_sq_done = sem("q_sq_done")
        k_sq_done = sem("k_sq_done")
        q_hi_done = sem("q_hi_done")
        q_lo_done = sem("q_lo_done")
        k_hi_done = sem("k_hi_done")
        k_lo_done = sem("k_lo_done")
        v_hi_done = sem("v_hi_done")
        v_lo_done = sem("v_lo_done")
        hssq_done = sem("hssq_done")
        hstd_done = sem("hstd_done")
        hinv_done = sem("hinv_done")
        kdiag_done = sem("kdiag_done")
        kn_done = sem("kn_done")
        kbc_done = sem("kbc_done")
        vt_done = sem("vt_done")
        score_done = sem("score_done")
        scaled_q_done = sem("scaled_q_done")
        biased_done = sem("biased_done")
        masked_done = sem("masked_done")
        exp_done = sem("exp_done")
        rowinv_done = sem("rowinv_done")
        prob_done = sem("prob_done")
        turned_done = sem("turned_done")
        pt_hi_done = sem("pt_hi_done")
        pt_lo_done = sem("pt_lo_done")
        pv_done = sem("pv_done")
        y_hi_done = sem("y_hi_done")
        y_lo_done = sem("y_lo_done")
        bd_hi_done = sem("bd_hi_done")
        bd_lo_done = sem("bd_lo_done")
        pad_done = sem("pad_done")
        conv_done = sem("conv_done")
        xc_hi_done = sem("xc_hi_done")
        xc_lo_done = sem("xc_lo_done")
        gelu_done = sem("gelu_done")
        gate_r_done = sem("gate_r_done")
        gate_i_done = sem("gate_i_done")
        sig_r_done = sem("sig_r_done")
        sig_i_done = sem("sig_i_done")
        tanh_done = sem("tanh_done")
        decay_done = sem("decay_done")
        sqa_done = sem("sqa_done")
        ix_done = sem("ix_done")
        mult2_done = sem("mult2_done")
        mult_done = sem("mult_done")
        u_done = sem("u_done")
        scan_done = sem("scan_done")
        ly_done = sem("ly_done")
        l_hi_done = sem("l_hi_done")
        l_lo_done = sem("l_lo_done")
        sp_done = sem("sp_done")
        sp_inv_done = sem("sp_inv_done")
        spe_done = sem("spe_done")
        table_mm = sem("table_mm")
        table_done = sem("table_done")
        skewed = sem("skewed")
        bias_landed = sem("bias_landed")
        wi_turned = sem("wi_turned")
        wi_done = sem("wi_done")
        ki_hi_done = sem("ki_hi_done")
        ki_lo_done = sem("ki_lo_done")
        ki_landed = sem("ki_landed")
        idx_done = sem("idx_done")
        relu_done = sem("relu_done")
        isc_done = sem("isc_done")
        top_done = sem("top_done")
        cut_done = sem("cut_done")
        sel_done = sem("sel_done")
        qi_hi_done = sem("qi_hi_done")
        qi_lo_done = sem("qi_lo_done")
        glu_sig_done = sem("glu_sig_done")
        glu_done = sem("glu_done")
        dw_done = sem("dw_done")
        c_hi_done = sem("c_hi_done")
        c_lo_done = sem("c_lo_done")
        mean_mm = sem("mean_mm")
        ln_add_done = sem("ln_add_done")
        cen_done = sem("cen_done")
        cen_sq_done = sem("cen_sq_done")
        var_mm = sem("var_mm")
        ln_std_done = sem("ln_std_done")
        ln_rcol_done = sem("ln_rcol_done")
        ln_diag_done = sem("ln_diag_done")
        ln_bc_done = sem("ln_bc_done")
        ln_inv_done = sem("ln_inv_done")
        scaled_done = sem("scaled_done")
        cy_done = sem("cy_done")
        ln_chain = sem("ln_chain")
        gq_done = sem("gq_done")
        causal_done = sem("causal_done")
        stored = sem("stored")

        block = ctx.enter_context(nc.Block())

        def xt_tile(d):
            return xt[:, ds(d * T, T)]

        def out_base(i):
            return UNIT_BASE[i + 1] - OUT_UNITS

        ps_norm = ps_unit[:, out_base(PHASES.index("odd")) % 2, :] if "odd" in PHASES else None

        def late(i, d, of_late, of_unit):
            if d < SPLIT_TILES - 1:
                return of_late, LATE_BASE[i] + d + 1
            return of_unit, out_base(i) + d + 2

        def late_bank(i, d):
            if d < SPLIT_TILES:
                return (ps_s, ps_t)[d // 2][:, d % 2, :]
            return ps_unit[:, (out_base(i) + d + 1) % 2, :]

        def gain(col, d):
            return vec[:, ds(COL[col] + d, 1)]

        @block.sync
        def _(sp):
            def load(n, slot):
                sp.dma_start(raw[:, slot, :], w_stream[ds(n, 1), :, :].rearrange("a p c -> (a p) c")).then_inc(w_landed[slot], 16)

            load(0, 0)
            for d in range(1, KT):
                sp.dma_start(xt_tile(d), xt_in[d]).then_inc(x_landed[d], 16)
                if d == 3:
                    load(1, 1)
            for n in range(2, RAW):
                load(n, n)
            sp.dma_start(ident[:, :], ident_in).then_inc(c_landed, 16)
            sp.dma_start(relb, relb_in).then_inc(c_landed, 16)
            sp.dma_start(onehot, onehot_in).then_inc(c_landed, 16)
            sp.dma_start(bd_raw, bd_in).then_inc(c_landed, 16)
            with sp.Fori(1, NUNITS // RAW) as i:
                for s in range(RAW):
                    sp.wait_ge(w_lo_done, i * RAW + (s - RAW + 1))
                    load(i * RAW + s, s)
            for n in range(NUNITS // RAW * RAW, NUNITS):
                sp.wait_ge(w_lo_done, n - RAW + 1)
                load(n, n % RAW)
            for d in range(KT):
                sp.wait_ge(x_added, X_BASE[-1] - KT + d + 1)
                sp.dma_start(out[d], xt_tile(d)).then_inc(stored, 16)
            sp.wait_ge(stored, 16 * KT)

        @block.gpsimd
        def _(pool):
            def constant(n, out, value):
                nc.gpsimd.memset(out, value).then_inc(const_done, 1)
                pool.wait_ge(const_done, n)

            sp_count = [0]

            def sp_step(ins):
                sp_count[0] += 1
                ins.then_inc(sp_done, 1)
                pool.wait_ge(sp_done, sp_count[0])

            def softplus():
                lam = vec[:, COL["lam"]:COL["lam"] + 4]
                e, z, z2, p = sp[:, 4:8], sp[:, 8:12], sp[:, 12:16], sp[:, 0:4]
                pool.wait_ge(spe_done, 2)
                sp_step(nc.gpsimd.tensor_scalar(z2, e, 2.0, None, ALU.add))
                pool.wait_ge(sp_inv_done, 1)
                sp_step(nc.gpsimd.tensor_tensor(z, z, e, ALU.mult))
                sp_step(nc.gpsimd.tensor_tensor(z2, z, z, ALU.mult))
                sp_step(nc.gpsimd.tensor_scalar(p, z2, 1.0 / 17, 1.0 / 15, ALU.mult, ALU.add))
                for c in (13, 11, 9, 7, 5, 3, 1):
                    sp_step(nc.gpsimd.tensor_tensor(p, p, z2, ALU.mult))
                    sp_step(nc.gpsimd.tensor_scalar(p, p, 1.0 / c, None, ALU.add))
                sp_step(nc.gpsimd.tensor_tensor(p, p, z, ALU.mult))
                sp_step(nc.gpsimd.tensor_scalar(z2, lam, -1.0, 0.0, ALU.mult, ALU.max))
                sp_step(nc.gpsimd.tensor_scalar(p, p, 2.0, None, ALU.mult))
                sp_step(nc.gpsimd.tensor_tensor(p, p, z2, ALU.add))
                sp_step(nc.gpsimd.tensor_scalar(c8[:, 0:4], p, LRU_C, None, ALU.mult))
                sp_step(nc.gpsimd.tensor_scalar(c8[:, 4:8], p, -LRU_C, None, ALU.mult))

            constant(1, ones[:, :], 1.0)
            constant(2, small[:, 0:1], EPS)
            constant(3, table[:, T:SKEW], NEG)
            constant(4, head_sel[:, :], 0.0)
            constant(5, head_row[:, :], 0.0)
            constant(6, head_row[:, HD:2 * HD], 1.0)
            for h in range(2):
                constant(7 + h, head_sel[h * HD:(h + 1) * HD, h:h + 1], 1.0)
            for b, buf in enumerate((v_hi, v_lo)):
                for par in range(2):
                    constant(9 + 2 * b + par, buf[:, par, :, HD:2 * HD].bitcast(F32), 0.0)
            pool.wait_ge(vec_landed, 16)
            for c, name in enumerate(("ev_q", "od_q")):
                nc.gpsimd.tensor_scalar(gq8[:, c:c + 1], gain(name, 0), HD ** -0.5, None, ALU.mult).then_inc(gq_done, 1)
            pool.wait_ge(gq_done, 2)
            softplus()
            pool.wait_ge(bd_hi_done, 1)
            nc.gpsimd.tensor_tensor(bdr_lo[:, :, :, :].rearrange("p a b c -> p (a b c)"), bd_raw,
                                    bdr_hi[:, :, :, :].rearrange("p a b c -> p (a b c)").bitcast(F32), ALU.subtract).then_inc(bd_lo_done, 1)
            if "odd" in PHASES:
                pool.wait_ge(unit_done, UNIT_BASE[PHASES.index("odd")])
                pool.wait_ge(unit_read, UNIT_BASE[PHASES.index("odd")])
                nc.gpsimd.memset(causal, 0.0).then_inc(causal_done, 1)
                pool.wait_ge(causal_done, 1)
                nc.gpsimd.affine_select(out=causal, in_=causal, compare_op=ALU.is_ge, fill=NEG, base=0,
                                        pattern=[[-1, P]], channel_multiplier=1).then_inc(causal_done, 1)

        @block.tensor
        def _(pe):
            def product(ps, lhs_hi, lhs_lo, rhs_hi, rhs_lo, first, last):
                pe.matmul(ps, lhs_hi, rhs_hi, start=first, stop=False)
                pe.matmul(ps, lhs_hi, rhs_lo, start=False, stop=False)
                return pe.matmul(ps, lhs_lo, rhs_hi, start=False, stop=last)

            def start_unit(n, is_first=False):
                pe.wait_ge(w_lo_done, n + 1)
                if not is_first:
                    pe.wait_ge(unit_read, n - 1)

            def blocks(s, ks, rhs_hi, rhs_lo, nk=KT, wait=None):
                for k in ks:
                    if wait:
                        wait(k)
                    w = slice(k * P, (k + 1) * P)
                    mm = product(ps_unit[:, s, :], w_hi[:, s, w], w_lo[:, s, w], rhs_hi(k), rhs_lo(k),
                                 k == 0, k == nk - 1)
                return mm

            def of_x(hi):
                return (lambda k: xs_hi[:, k, :]) if hi else (lambda k: xs_lo[:, k, :])

            def of_a(hi):
                buf = a_hi if hi else a_lo
                return lambda k: buf[:, k * T:(k + 1) * T]

            def first_units(i):
                n = UNIT_BASE[i]
                start_unit(n, is_first=n < 2)
                blocks(n % 2, range(KT), of_x(1), of_x(0),
                       wait=lambda k: pe.wait_ge(x_lo_done, KT * i + k + 1)).then_inc(unit_done, 1)
                pe.wait_ge(const_done, 2)
                pe.wait_ge(acc_done, KT * (i + 1))
                for t in range(TT):
                    mm = pe.matmul(ps_misc[:, t:t + 1], acc[:, t * P:(t + 1) * P], ones[:, 0:1], start=True, stop=True)
                mm.then_inc(ssq_done, 1)
                n += 1
                start_unit(n, is_first=n < 2)
                blocks(n % 2, range(KT // 2), of_x(1), of_x(0))
                pe.wait_ge(diag_done, i + 1)
                pe.matmul(ps_misc[:, :], ones[:, :], diag[:, :], start=True, stop=True).then_inc(rbc_done, 1)
                blocks(n % 2, range(KT // 2, KT), of_x(1), of_x(0)).then_inc(unit_done, 1)

            def x_unit(n, s):
                start_unit(n)
                blocks(s, range(KT), of_x(1), of_x(0)).then_inc(unit_done, 1)

            def ffn(i):
                n0, tile0 = UNIT_BASE[i], FFN_BASE[i]
                first_units(i)
                for k in (2, 3):
                    x_unit(n0 + k, (n0 + k) % 2)
                if i == 0:
                    pe.wait_ge(c_landed, 16 * 4)
                    pe.matmul(ps_y[0:HEADS, :], relb, onehot, start=True, stop=True).then_inc(table_mm, 1)
                n, tile = n0, tile0
                for g, tiles in enumerate(GROUPS):
                    with pe.Fori(1 if g == 0 else 0, tiles // 2) as it:
                        for k in range(4):
                            x_unit(it * 4 + (n + k), (n0 + k) % 2)
                    n, tile = n + 2 * tiles, tile + tiles
                    with pe.Fori(0, KT // 4) as it:
                        for k in range(4):
                            start_unit(it * 4 + (n + k))
                            blocks((n0 + k) % 2, range(tiles), of_a(1), of_a(0), nk=tiles,
                                   wait=lambda f: pe.wait_ge(a_lo_done, tile - tiles + f + 1) if k == 0 else None
                                   ).then_inc(unit_done, 1)
                    n += KT

            def head_ssq(a):
                pe.wait_ge(q_sq_done, a + 1)
                pe.wait_ge(k_sq_done, a + 1)
                if a:
                    pe.wait_ge(kn_done, a)
                for m in range(2):
                    for t in range(TT):
                        mm = pe.matmul(ps_misc[:, (m * TT + t) * 2:(m * TT + t) * 2 + 2],
                                       sqb[:, m, t * P:(t + 1) * P], head_sel[:, :], start=True, stop=True)
                mm.then_inc(hssq_done, 1)

            def turn_v(a, n):
                pe.wait_ge(unit_read, n + 1)
                pe.wait_ge(hstd_done, a + 1)
                for t in range(TT):
                    mm = pe.transpose(ps_misc[:, t * P:(t + 1) * P], t2[:, t * P:(t + 1) * P], ident[:, :])
                mm.then_inc(vt_done, 1)

            def spread_k(a):
                pe.wait_ge(kdiag_done, a + 1)
                pe.wait_ge(v_lo_done, a + 1)
                pe.matmul(ps_misc[:, :], head_row[:, HD:3 * HD], diag[:, :], start=True, stop=False)
                pe.matmul(ps_misc[:, :], head_row[:, 0:2 * HD], acc[:, :], start=False, stop=True).then_inc(kbc_done, 1)

            def score(a, r):
                R, h, n = 8 * a + r, r // 4, (r % 4 + 1) * P
                if r == 0:
                    pe.wait_ge(k_lo_done, a + 1)
                    pe.wait_ge(q_lo_done, a + 1)
                if R >= 2:
                    pe.wait_ge(scaled_q_done, R - 1)
                f, t = slice(h * HD, (h + 1) * HD), slice(n - P, n)
                product(ps_s[:, R % 2, 0:n], q_hi[f, a % 2, t], q_lo[f, a % 2, t], k_hi[f, a % 2, 0:n],
                        k_lo[f, a % 2, 0:n], True, True).then_inc(score_done, 1)

            def turn(a, r):
                R = 8 * a + r
                pe.wait_ge(prob_done, R + 1)
                if R >= 2:
                    pe.wait_ge(pt_lo_done, R - 1)
                for j in range(r % 4 + 1):
                    mm = pe.transpose(ps_t[:, R % 2, j * P:(j + 1) * P], probs[:, R % 2, j * P:(j + 1) * P], ident[:, :])
                mm.then_inc(turned_done, 1)

            def weigh(a, h):
                pe.wait_ge(pt_lo_done, 8 * a + 4 * h + 4)
                if h == 0 and a < 4:
                    pe.wait_ge(sig_i_done, a + 1)
                elif h == 0:
                    pe.wait_ge(y_lo_done, a)
                for j in range(TT):
                    w = slice(h * HD, h * HD + P)
                    mm = product(ps_y[:, j * P:T], v_hi[:, a % 2, j, w], v_lo[:, a % 2, j, w],
                                 pt_hi[:, j, j * P:T], pt_lo[:, j, j * P:T], h == 0 and j == 0, h == 1 and j == TT - 1)
                mm.then_inc(pv_done, 1)

            def attend(a, p, first):
                if p == 0 and not first:
                    weigh(a - 1, 1)
                if p == 3:
                    weigh(a, 0)
                for r in (2 * p - 2, 2 * p - 1):
                    if r >= 0:
                        turn(a, r)
                if p < 4:
                    score(a, 2 * p)
                    score(a, 2 * p + 1)

            def lru_gate(j, which):
                if which == 0:
                    pe.wait_ge(xc_lo_done, j + 1)
                    if j:
                        pe.wait_ge(y_lo_done, j)
                    pe.wait_ge(bd_lo_done, 1)
                else:
                    pe.wait_ge(sig_r_done, j + 1)
                product(ps_y[:, :], bdr_hi[:, which, j, :], bdr_lo[:, which, j, :], xc_hi[:, :], xc_lo[:, :],
                        True, True).then_inc(gate_r_done if which == 0 else gate_i_done, 1)

            def out_blocks(ps, n, at, i, ks, first, last):
                for p, k in enumerate(ks):
                    if n == out_base(i) and k < 4:
                        pe.wait_ge(l_lo_done, k + 1 if PHASES[i] == "even" else 4 + k + 1)
                    w, y = slice((at + p) * P, (at + p + 1) * P), slice(k * T, (k + 1) * T)
                    mm = product(ps, w_hi[:, n % 2, w], w_lo[:, n % 2, w], a_hi[:, y], a_lo[:, y],
                                 first and p == 0, last and p == len(ks) - 1)
                return mm

            def mix_out(i, a):
                is_even = PHASES[i] == "even"
                early, late_ks, n = EARLY[PHASES[i]], LATE[PHASES[i]], out_base(i)
                if not is_even:
                    pe.wait_ge(ln_inv_done, 1)
                for u in range(5):
                    if is_even and u == 1:
                        lru_gate(3, 0)
                    m, ready = n + u, READY[PHASES[i]] if u == 0 else 0
                    if ready:
                        start_unit(m)
                        out_blocks(ps_unit[:, m % 2, :], m, 0, i, early[:ready], True, False)
                    attend(a, u, False)
                    if is_even and u == 1:
                        lru_gate(3, 1)
                    if u < SPLIT_TILES:
                        if not ready:
                            start_unit(m)
                        if ready < len(early) - 1:
                            out_blocks(ps_unit[:, m % 2, :], m, ready, i, early[ready:-1], not ready, False)
                        pe.wait_ge(y_lo_done, a)
                        out_blocks(ps_unit[:, m % 2, :], m, len(early) - 1, i, early[-1:], False, True).then_inc(unit_done, 1)
                    else:
                        start_unit(m + 1)
                        out_blocks(ps_unit[:, (m + 1) % 2, :], m + 1, 0, i, early, True, False)
                weigh(a, 1)
                if is_even:
                    pe.wait_ge(l_lo_done, 4)
                pe.wait_ge(y_lo_done, a + 1)
                m = n + SPLIT_TILES
                for d in range(SPLIT_TILES):
                    out_blocks(late_bank(i, d), m, d * len(late_ks), i, late_ks, True, True).then_inc(
                        late(i, d, late_done, unit_done)[0], 1)
                for m in range(n + SPLIT_TILES + 1, n + OUT_UNITS):
                    if m > n + SPLIT_TILES + 1:
                        start_unit(m)
                        out_blocks(ps_unit[:, m % 2, :], m, 0, i, early, True, False)
                    out_blocks(ps_unit[:, m % 2, :], m, len(early), i, late_ks, False, True).then_inc(unit_done, 1)

            def even(i):
                n0 = UNIT_BASE[i]
                for it in range(4):
                    for u in range(5):
                        n = n0 + 5 * it + u
                        if it == 0 and u == 0:
                            first_units(i)
                        elif it or u > 1:
                            if it and u == 1:
                                lru_gate(it - 1, 0)
                            x_unit(n, n % 2)
                        if it:
                            if u == 1:
                                lru_gate(it - 1, 1)
                            attend(it - 1, u, it == 1)
                        if u == 2:
                            head_ssq(it)
                        if u == 3:
                            turn_v(it, n0 + 5 * it + 2)
                        if u == 4:
                            spread_k(it)
                mix_out(i, 3)

            def index_row(q):
                t, h = 1 + q // HEADS, q % HEADS
                n = (t + 1) * P
                if q == 0:
                    pe.wait_ge(qi_lo_done, 4)
                    pe.wait_ge(ki_landed, 32)
                if q >= 2:
                    pe.wait_ge(relu_done, q - 1)
                else:
                    pe.wait_ge(scaled_q_done, 32)
                f = slice(h % 2 * HD, h % 2 * HD + HD)
                qi = slice((4 + h // 2) * T + t * P, (4 + h // 2) * T + (t + 1) * P)
                product(ps_s[:, q % 2, 0:n], a_hi[f, qi], a_lo[f, qi], ki_hi[f, 0:n], ki_lo[f, 0:n],
                        True, True).then_inc(idx_done, 1)

            def odd(i):
                n0 = UNIT_BASE[i]
                first_units(i)
                for u in range(2, IDX_IN):
                    x_unit(n0 + u, (n0 + u) % 2)
                pe.wait_ge(unit_read, n0 + 1)
                pe.wait_ge(rstd_done, i + 1)
                for t in range(TT):
                    mm = pe.transpose(ps_misc[:, t * P:(t + 1) * P], t0[:, t * P:(t + 1) * P], ident[:, :])
                mm.then_inc(wi_turned, 1)
                for m in range(GLU_IN):
                    x_unit(n0 + IDX_IN + m, (n0 + IDX_IN + m) % 2)
                    if m < 4:
                        for q in range(6 * m, 6 * m + 6):
                            index_row(q)
                for j in range(2):
                    for c in range(CONV_UNITS):
                        conv_unit(j, c, n0 + IDX_IN + GLU_IN + CONV_UNITS * j + c)
                for it in range(4):
                    for u in range(5):
                        n = n0 + ODD_BASE[it] + u
                        if u < 3:
                            x_unit(n, n % 2)
                        elif u < ODD_IN[it]:
                            conv_unit(it + 1, u - 3, n)
                        if it == 3 and u == 3:
                            pe.wait_ge(ln_std_done, 1)
                        if it:
                            attend(4 + it - 1, u, it == 1)
                        if it == 3:
                            conv_norm(u)
                        if u == 2:
                            head_ssq(4 + it)
                        if u == 3:
                            turn_v(4 + it, n0 + ODD_BASE[it] + 2)
                        if u == 4:
                            spread_k(4 + it)
                mix_out(i, 7)

            def conv_unit(j, c, n):
                start_unit(n)
                if c == 0:
                    pe.wait_ge(c_lo_done, j + 1)
                at = j % 2 * 2 * T + KT * c
                blocks(n % 2, range(KT), lambda k: a_hi[:, at + k:at + k + T], lambda k: a_lo[:, at + k:at + k + T]
                       ).then_inc(unit_done, 1)

            def conv_norm(u):
                if u == 0:
                    pe.wait_ge(ln_add_done, 1)
                    pe.wait_ge(kn_done, 7)
                    pe.matmul(ps_misc[:, :], ones[:, :], branch_sum, start=True, stop=True).then_inc(mean_mm, 1)
                if u == 2:
                    pe.wait_ge(ln_add_done, 2)
                    pe.wait_ge(y_lo_done, 6)
                    for t in range(TT):
                        mm = pe.matmul(ps_y[:, t:t + 1], branch_sum[:, t * P:(t + 1) * P], ones[:, 0:1], start=True, stop=True)
                    mm.then_inc(var_mm, 1)
                    pe.wait_ge(cen_done, 4)
                if u == 3:
                    pe.wait_ge(ln_diag_done, 1)
                    pe.wait_ge(unit_read, out_base(PHASES.index("odd")) - 1)
                    pe.matmul(ps_norm, ones[:, :], branch_diag, start=True, stop=True).then_inc(ln_bc_done, 1)

            for i, phase in enumerate(PHASES):
                {"ffn": ffn, "even": even, "odd": odd}[phase](i)

        @block.scalar
        def _(act):
            def split_hi(n, slot, s, is_first=False):
                act.wait_ge(w_landed[slot], 16 * (n // RAW + 1) if type(n) is int else (n - slot) * (16 // RAW) + 16)
                if not is_first:
                    act.wait_ge(unit_done, n - 1)
                act.activation(w_hi[:, s, :], raw[:, slot, :], ACT.Copy).then_inc(w_hi_done, 1)

            def hi_ahead(n, k, n0):
                split_hi(n, (n0 + k) % RAW, (n0 + k) % 2)

            def split_x(i, d):
                act.activation(xs_hi[:, d, :], xt_tile(d), ACT.Copy, scale=gain("norm", i * KT + d)).then_inc(x_hi_done, 1)
                if i * KT + d >= 2:
                    act.wait_ge(acc_done, i * KT + d - 1)
                act.activation(sqb[:, d % 2, :], xt_tile(d), ACT.Square).then_inc(sq_done, 1)

            def norm_std(i):
                act.wait_ge(ssq_done, i + 1)
                act.activation(small[:, 1:1 + TT], ps_misc[:, 0:TT], ACT.Sqrt, bias=small[:, 0:1],
                               scale=1.0 / D).then_inc(std_done, 1)

            def silu(n, tile):
                act.wait_ge(unit_read, n + 1)
                act.activation(t1[:, :], t0[:, :], ACT.Silu).then_inc(silu_done, 1)

            def hidden_hi(n, j):
                act.wait_ge(unit_read, n + 1)
                act.activation(a_hi[:, ds(j * T, T)], t2[:, :], ACT.Copy).then_inc(a_hi_done, 1)

            def pair(n, j, tile, n0, norm=None):
                for m in range(2):
                    hi_ahead(n + (2 * m + 2), 2 * m + 2, n0)
                    if norm is not None and m == 0:
                        norm_std(norm)
                    silu(n + 2 * m, tile + m)
                    hi_ahead(n + (2 * m + 3), 2 * m + 3, n0)
                    hidden_hi(n + (2 * m + 1), j + m)

            def ffn(i):
                n0, tile0 = UNIT_BASE[i], FFN_BASE[i]
                pair(n0, 0, tile0, n0, norm=i)
                n, tile = n0, tile0
                for g, tiles in enumerate(GROUPS):
                    with act.Fori(1 if g == 0 else 0, tiles // 2) as it:
                        pair(it * 4 + n, it * 2, it * 2 + tile, n0)
                    n, tile = n + 2 * tiles, tile + tiles
                    if i == 0:
                        prepare(g)
                    if g < len(GROUPS) - 1:
                        with act.Fori(0, KT // 4) as it:
                            for k in range(4):
                                hi_ahead(it * 4 + (n + k + 2), k + 2, n0)
                    else:
                        for d in range(KT):
                            if n + d + 2 < NUNITS:
                                split_hi(n + d + 2, (n + d + 2) % RAW, (n + d + 2) % 2)
                            if i + 1 < len(PHASES):
                                act.wait_ge(x_added, X_BASE[i + 1] - KT + d + 1)
                                split_x(i + 1, d)
                    n += KT

            def square_q(a, n, m):
                act.wait_ge(unit_read, n + 1)
                if a:
                    act.wait_ge(hssq_done, a)
                act.activation(sqb[:, m, :], (t0, t1)[m][:, :], ACT.Square).then_inc((q_sq_done, k_sq_done)[m], 1)

            def q_high(a):
                if a >= 2:
                    act.wait_ge(score_done, 8 * (a - 1))
                act.activation(q_hi[:, a % 2, :], t0[:, :], ACT.Copy, scale=gq8[:, a // 4:a // 4 + 1]).then_inc(q_hi_done, 1)

            def head_std(a):
                act.wait_ge(hssq_done, a + 1)
                if a:
                    act.wait_ge(hinv_done, a)
                act.activation(hstd[:, :], ps_misc[:, 0:16], ACT.Sqrt, bias=small[:, 0:1], scale=1.0 / HD).then_inc(hstd_done, 1)

            def v_high(a):
                act.wait_ge(vt_done, a + 1)
                if a >= 2:
                    act.wait_ge(pv_done, 2 * (a - 1))
                v = ps_misc[:, :].rearrange("p (t f) -> p t f", f=P)
                for h in range(2):
                    ins = act.activation(v_hi[:, a % 2, :, 2 * h * HD:2 * h * HD + HD], v[:, :, h * HD:(h + 1) * HD], ACT.Copy)
                ins.then_inc(v_hi_done, 1)

            def k_high(a):
                act.wait_ge(kn_done, a + 1)
                if a >= 2:
                    act.wait_ge(score_done, 8 * (a - 1))
                act.activation(k_hi[:, a % 2, :], t1[:, :], ACT.Copy).then_inc(k_hi_done, 1)

            def scale_scores(a, r):
                R, h, t = 8 * a + r, r // 4, r % 4
                n, c = (t + 1) * P, 2 * t + h
                act.wait_ge(score_done, R + 1)
                act.wait_ge(hinv_done, a + 1)
                if R >= 2:
                    act.wait_ge(turned_done, R - 1)
                act.activation(probs[:, R % 2, 0:n], ps_s[:, R % 2, 0:n], ACT.Copy,
                               scale=hinv[:, a % 2, c:c + 1]).then_inc(scaled_q_done, 1)

            def exp(a, r):
                R, n = 8 * a + r, (r % 4 + 1) * P
                act.wait_ge(biased_done, R + 1)
                p = probs[:, R % 2, 0:n]
                act.activation(p, p, ACT.Exp, scale=-1.0, bias=negmax[:, R % 2:R % 2 + 1], accum_out=rowsum[:, R % 2:R % 2 + 1]).then_inc(exp_done, 1)

            def pt_high(a, r):
                R, n = 8 * a + r, r % 4 + 1
                act.wait_ge(turned_done, R + 1)
                act.activation(pt_hi[:, 0:n, (n - 1) * P:n * P],
                               ps_t[:, R % 2, 0:n * P].rearrange("p (j t) -> p j t", t=P), ACT.Copy).then_inc(pt_hi_done, 1)

            def y_high(a):
                act.wait_ge(pv_done, 2 * (a + 1))
                act.activation(a_hi[:, (4 + a % 4) * T:(5 + a % 4) * T], ps_y[:, :], ACT.Copy).then_inc(y_hi_done, 1)

            def attend(a, p, first):
                if p == 0 and not first:
                    y_high(a - 1)
                for r in (2 * p - 2, 2 * p - 1):
                    if r >= 0:
                        pt_high(a, r)
                if p < 4:
                    scale_scores(a, 2 * p)
                    scale_scores(a, 2 * p + 1)
                    exp(a, 2 * p)
                    exp(a, 2 * p + 1)

            def pair_in(a, u, n):
                if u == 0:
                    square_q(a, n, 0)
                    q_high(a)
                if u == 1:
                    square_q(a, n, 1)
                if u == 2:
                    head_std(a)
                if u == 3:
                    v_high(a)
                if u == 4:
                    k_high(a)

            def gate_sigmoid(j, which):
                act.wait_ge((gate_r_done, gate_i_done)[which], j + 1)
                act.activation((ra, ri)[which], ps_y[:, :], ACT.Sigmoid,
                               bias=gain(("ra_b", "ix_b")[which], j)).then_inc((sig_r_done, sig_i_done)[which], 1)

            def lru(j, u, n):
                if 0 <= j < 4:
                    if u == 1:
                        act.wait_ge(sig_r_done, j + 1)
                        act.activation(half[:, :], ra, ACT.Tanh, scale=c8[:, j:j + 1]).then_inc(tanh_done, 1)
                        act.wait_ge(tanh_done, j + 1)
                        act.activation(ra, ra, ACT.Exp, scale=c8[:, 4 + j:5 + j]).then_inc(decay_done, 1)
                        act.wait_ge(decay_done, j + 1)
                        act.activation(hh, ra, ACT.Square).then_inc(sqa_done, 1)
                    if u == 2:
                        act.wait_ge(mult2_done, j + 1)
                        act.activation(half[:, :], half[:, :], ACT.Sqrt).then_inc(mult_done, 1)
                        g = gelu[j % 2]
                        act.activation(g, g, ACT.Gelu_apprx_tanh).then_inc(gelu_done, 1)
                    if u == 3:
                        act.wait_ge(ly_done, j + 1)
                        act.activation(a_hi[:, j * T:(j + 1) * T], hh, ACT.Copy).then_inc(l_hi_done, 1)
                if j < 3 and u == 4:
                    act.wait_ge(conv_done, 4 * (j + 2))
                    act.activation(xc_hi[:, :], xc, ACT.Copy).then_inc(xc_hi_done, 1)

            def prepare(step):
                if step == 0:
                    act.activation(bdr_hi[:, :, :, :].rearrange("p a b c -> p (a b c)"), bd_raw, ACT.Copy).then_inc(bd_hi_done, 1)
                    act.wait_ge(table_mm, 1)
                    act.activation(table[:, 0:T], ps_y[0:HEADS, :], ACT.Copy).then_inc(table_done, 1)
                    act.wait_ge(table_done, 1)
                    act.dma_start(skew, table.rearrange("h (o y) -> h o y", o=1).to_broadcast([HEADS, P, SKEW])).then_inc(skewed, 16)
                if step == 1:
                    act.wait_ge(skewed, 16)
                    act.dma_start(bias_t[:, :, :], skew.rearrange("h p y -> h (p y)")[:, P - 1:P - 1 + P * (SKEW - 1)].rearrange(
                        "h (p y) -> p h y", y=SKEW - 1)[:, :, 0:T]).then_inc(bias_landed, 16)

            def mix_out(i, a):
                n = out_base(i)
                for u in range(5):
                    if PHASES[i] == "even" and u == 1:
                        gate_sigmoid(3, 0)
                        gate_sigmoid(3, 1)
                    attend(a, u, False)
                    if u < SPLIT_TILES:
                        m = n + u + 2
                        split_hi(m, m % RAW, m % 2)
                    if PHASES[i] == "even":
                        lru(3, u, n)
                y_high(a)
                for d in range(KT):
                    if d == 0 or d >= SPLIT_TILES:
                        m = n + 3 + max(d, SPLIT_TILES - 1)
                        split_hi(m, m % RAW, m % 2)
                    act.wait_ge(*late(i, d, late_read, unit_read))
                    split_x(i + 1, d)

            def even(i):
                n0 = UNIT_BASE[i]
                for it in range(4):
                    for u in range(5):
                        n = n0 + 5 * it + u
                        if it and u == 1:
                            gate_sigmoid(it - 1, 0)
                        split_hi(n + 2, (n + 2) % RAW, (n + 2) % 2)
                        if it and u == 1:
                            gate_sigmoid(it - 1, 1)
                        if it == 0 and u == 0:
                            norm_std(i)
                        if it:
                            attend(it - 1, u, it == 1)
                        pair_in(it, u, n)
                        lru(it - 1, u, n)
                mix_out(i, 3)

            def index_row(q):
                n = (2 + q // HEADS) * P
                act.wait_ge(idx_done, q + 1)
                if q >= 2:
                    act.wait_ge(isc_done, q - 1)
                act.activation(relu[q % 2][:, 0:n], ps_s[:, q % 2, 0:n], ACT.Relu).then_inc(relu_done, 1)

            def odd(i):
                n0 = UNIT_BASE[i]
                for u in range(IDX_IN):
                    n = n0 + u
                    split_hi(n + 2, (n + 2) % RAW, (n + 2) % 2)
                    if u == 0:
                        norm_std(i)
                        act.wait_ge(unit_read, n + 1)
                        act.activation(ki_hi[0:HD, :], t0[0:HD, :], ACT.Copy).then_inc(ki_hi_done, 1)
                        act.wait_ge(ki_lo_done, 1)
                        act.dma_start(ki_hi[HD:P, :].bitcast(F32), ki_hi[0:HD, :].bitcast(F32)).then_inc(ki_landed, 16)
                        act.dma_start(ki_lo[HD:P, :].bitcast(F32), ki_lo[0:HD, :].bitcast(F32)).then_inc(ki_landed, 16)
                    else:
                        act.wait_ge(unit_read, n + 1)
                        act.activation(a_hi[:, (3 + u) * T:(4 + u) * T], t1[:, :], ACT.Copy).then_inc(qi_hi_done, 1)
                for m in range(GLU_IN):
                    n = n0 + IDX_IN + m
                    split_hi(n + 2, (n + 2) % RAW, (n + 2) % 2)
                    if m % 2:
                        act.wait_ge(unit_read, n + 1)
                        act.activation(t2[:, :], t2[:, :], ACT.Sigmoid).then_inc(glu_sig_done, 1)
                    if m < 4:
                        for q in range(6 * m, 6 * m + 6):
                            index_row(q)
                    if m == 4 or m == 5:
                        conv_high(m - 4)
                for n in range(n0 + IDX_IN + GLU_IN, n0 + ODD_FIRST):
                    split_hi(n + 2, (n + 2) % RAW, (n + 2) % 2)
                for it in range(4):
                    for u in range(5):
                        n = n0 + ODD_BASE[it] + u
                        if u < ODD_IN[it]:
                            split_hi(n + 2, (n + 2) % RAW, (n + 2) % 2)
                        if u == 1 and it in (1, 2):
                            conv_high(it + 1)
                        if it == 3 and u == 1:
                            conv_norm(u)
                        if it:
                            attend(4 + it - 1, u, it == 1)
                        pair_in(4 + it, u, n)
                        if it == 3 and u > 1:
                            conv_norm(u)
                mix_out(i, 7)

            def conv_high(j):
                act.wait_ge(glu_done, j + 1)
                if j < 2:
                    act.wait_ge(pad_done, 5)
                at = j % 2 * 2 * T
                act.activation(a_hi[:, at:at + T + DW_TAPS - 1], c_pad[j], ACT.Copy).then_inc(c_hi_done, 1)

            def conv_norm(u):
                if u == 1:
                    for c in range(4):
                        act.wait_ge(cen_done, c + 1)
                        act.activation(squares[c], cv[c], ACT.Square).then_inc(cen_sq_done, 1)
                if u == 2:
                    act.wait_ge(var_mm, 1)
                    act.activation(small[:, 1:1 + TT], ps_y[:, 0:TT], ACT.Sqrt, bias=small[:, 0:1], scale=1.0 / (4 * P)).then_inc(ln_std_done, 1)
                if u == 3:
                    act.wait_ge(ln_bc_done, 1)
                    act.activation(branch_inv, ps_norm, ACT.Copy).then_inc(ln_inv_done, 1)
                if u == 4:
                    for c in range(5):
                        if c < 4:
                            act.wait_ge(scaled_done, c + 1)
                            act.activation(cv[c], cv[c], ACT.Silu, bias=gain("ln_b", c)).then_inc(cy_done, 1)
                        if c:
                            act.wait_ge(cy_done, c)
                            act.activation(a_hi[:, (c - 1) * T:c * T], cv[c - 1], ACT.Copy).then_inc(l_hi_done, 1)

            act.dma_start(vec[:, :], vec_in).then_inc(vec_landed, 16)
            act.dma_start(xt_tile(0), xt_in[0]).then_inc(x_landed[0], 16)
            act.wait_ge(vec_landed, 16)
            for d in range(KT):
                if d < 2:
                    split_hi(d, d, d, is_first=True)
                act.wait_ge(x_landed[d], 16)
                split_x(0, d)
            act.activation(sp[:, 0:4], vec[:, COL["lam"]:COL["lam"] + 4], ACT.Abs).then_inc(spe_done, 1)
            act.wait_ge(spe_done, 1)
            act.activation(sp[:, 4:8], sp[:, 0:4], ACT.Exp, scale=-1.0).then_inc(spe_done, 1)
            act.wait_ge(const_done, 12)
            act.wait_ge(c_landed, 16 * 4)
            for i, phase in enumerate(PHASES):
                {"ffn": ffn, "even": even, "odd": odd}[phase](i)

        @block.vector
        def _(dve):
            def split_lo(n, slot, s):
                dve.wait_ge(w_hi_done, n + 1)
                dve.tensor_tensor(w_lo[:, s, :], raw[:, slot, :], w_hi[:, s, :].bitcast(F32),
                                  ALU.subtract).then_inc(w_lo_done, 1)

            def lo_ahead(n, k, n0):
                split_lo(n, (n0 + k) % RAW, (n0 + k) % 2)

            def split_x(i, d):
                dve.wait_ge(x_hi_done, i * KT + d + 1)
                dve.scalar_tensor_tensor(xs_lo[:, d, :], xt_tile(d), gain("norm", i * KT + d),
                                         xs_hi[:, d, :].bitcast(F32), ALU.mult, ALU.subtract).then_inc(x_lo_done, 1)
                dve.wait_ge(sq_done, i * KT + d + 1)
                if d == 0:
                    if i:
                        dve.wait_ge(ssq_done, i)
                    dve.tensor_copy(acc[:, :], sqb[:, 0, :]).then_inc(acc_done, 1)
                else:
                    dve.wait_ge(acc_done, i * KT + d)
                    dve.tensor_tensor(acc[:, :], acc[:, :], sqb[:, d % 2, :], ALU.add).then_inc(acc_done, 1)

            ident_4 = ident[:, :].rearrange("p (o c) -> p o c", o=1).to_broadcast([P, TT, P])

            def blocks_of(x):
                return x.rearrange("p (t c) -> p t c", c=P)

            def column_4(x):
                return x.rearrange("p (t o) -> p t o", o=1).to_broadcast([P, TT, P])

            def norm_diag(i):
                dve.wait_ge(std_done, i + 1)
                dve.reciprocal(rcol[:, :], small[:, 1:1 + TT]).then_inc(rcol_done, 1)
                dve.wait_ge(rcol_done, i + 1)
                if i == 0:
                    dve.wait_ge(c_landed, 16 * 4)
                dve.tensor_tensor(blocks_of(diag[:, :]), ident_4, column_4(rcol[:, 0:TT]), ALU.mult).then_inc(diag_done, 1)

            def norm_rstd(i):
                dve.wait_ge(rbc_done, i + 1)
                dve.tensor_copy(rstd[:, :], ps_misc[:, :]).then_inc(rstd_done, 1)
                dve.wait_ge(rstd_done, i + 1)
                dve.tensor_scalar(half[:, :], rstd[:, :], 0.5, None, ALU.mult).then_inc(half_done, 1)

            def gate(n, s, tile):
                dve.wait_ge(unit_done, n + 1)
                if type(tile) is not int or tile > 0:
                    dve.wait_ge(silu_done, tile)
                dve.tensor_tensor(t0[:, :], ps_unit[:, s, :], rstd[:, :], ALU.mult).then_inc(unit_read, 1)

            def up(n, s, tile):
                dve.wait_ge(unit_done, n + 1)
                dve.wait_ge(silu_done, tile + 1)
                if type(tile) is not int or tile > 0:
                    dve.wait_ge(a_hi_done, tile)
                dve.tensor_tensor(t2[:, :], ps_unit[:, s, :], t1[:, :], ALU.mult).then_inc(unit_read, 1)

            def hidden_lo(j, tile):
                dve.wait_ge(a_hi_done, tile + 1)
                dve.tensor_tensor(a_lo[:, ds(j * T, T)], t2[:, :], a_hi[:, ds(j * T, T)].bitcast(F32),
                                  ALU.subtract).then_inc(a_lo_done, 1)

            def pair(n, j, tile, n0, norm=None):
                for m in range(2):
                    if norm is not None and m == 0:
                        lo_ahead(n + 2, 2, n0)
                        norm_diag(norm)
                        norm_rstd(norm)
                        dve.wait_ge(half_done, norm + 1)
                    gate(n + 2 * m, (n0 + 2 * m) % 2, tile + m)
                    if norm is None or m == 1:
                        lo_ahead(n + (2 * m + 2), 2 * m + 2, n0)
                    up(n + (2 * m + 1), (n0 + 2 * m + 1) % 2, tile + m)
                    lo_ahead(n + (2 * m + 3), 2 * m + 3, n0)
                    hidden_lo(j + m, tile + m)

            def add_down(n, s, d, x_count):
                dve.wait_ge(unit_done, n + 1)
                if type(x_count) is not int or x_count > 0:
                    dve.wait_ge(x_added, x_count)
                dve.tensor_tensor(t0[:, :], ps_unit[:, s, :], half[:, :], ALU.mult).then_inc(unit_read, 1)
                dve.wait_ge(unit_read, n + 1)
                dve.tensor_tensor(xt_tile(d), xt_tile(d), t0[:, :], ALU.add).then_inc(x_added, 1)

            def ffn(i):
                n0, tile0 = UNIT_BASE[i], FFN_BASE[i]
                pair(n0, 0, tile0, n0, norm=i)
                n, tile = n0, tile0
                for g, tiles in enumerate(GROUPS):
                    with dve.Fori(1 if g == 0 else 0, tiles // 2) as it:
                        pair(it * 4 + n, it * 2, it * 2 + tile, n0)
                    n, tile = n + 2 * tiles, tile + tiles
                    dve.wait_ge(silu_done, tile)
                    if g < len(GROUPS) - 1:
                        with dve.Fori(0, KT // 4) as it:
                            for k in range(4):
                                add_down(it * 4 + (n + k), (n0 + k) % 2, it * 4 + k, it * 4 + (X_BASE[i] + g * KT + k))
                                lo_ahead(it * 4 + (n + k + 2), k + 2, n0)
                        dve.wait_ge(x_added, X_BASE[i] + (g + 1) * KT)
                    else:
                        for d in range(KT):
                            add_down(n + d, (n + d) % 2, d, X_BASE[i] + g * KT + d)
                            if n + d + 2 < NUNITS:
                                split_lo(n + d + 2, (n + d + 2) % RAW, (n + d + 2) % 2)
                            if i + 1 < len(PHASES):
                                split_x(i + 1, d)
                    n += KT

            def q_scaled(a, n):
                dve.wait_ge(unit_done, n + 1)
                if a:
                    dve.wait_ge(q_lo_done, a)
                dve.tensor_tensor(t0[:, :], ps_unit[:, n % 2, :], rstd[:, :], ALU.mult).then_inc(unit_read, 1)

            def q_low(a):
                dve.wait_ge(q_hi_done, a + 1)
                dve.scalar_tensor_tensor(q_lo[:, a % 2, :], t0[:, :], gq8[:, a // 4:a // 4 + 1],
                                         q_hi[:, a % 2, :].bitcast(F32), ALU.mult, ALU.subtract).then_inc(q_lo_done, 1)

            def k_scaled(a, n):
                dve.wait_ge(unit_done, n + 1)
                if a:
                    dve.wait_ge(k_lo_done, a)
                dve.tensor_tensor(t1[:, :], ps_unit[:, n % 2, :], rstd[:, :], ALU.mult).then_inc(unit_read, 1)

            def v_scaled(a, n):
                dve.wait_ge(unit_done, n + 1)
                if a:
                    dve.wait_ge(vt_done, a)
                dve.tensor_tensor(t2[:, :], ps_unit[:, n % 2, :], rstd[:, :], ALU.mult).then_inc(unit_read, 1)

            def head_inv(a):
                dve.wait_ge(hstd_done, a + 1)
                if a >= 2:
                    dve.wait_ge(scaled_q_done, 8 * (a - 1))
                dve.reciprocal(hinv[:, a % 2, :], hstd[:, :]).then_inc(hinv_done, 1)
                dve.wait_ge(hinv_done, a + 1)
                if a:
                    dve.wait_ge(kbc_done, a)
                for h in range(2):
                    inv = hinv[:, a % 2, 2 * TT:].rearrange("p (t h) -> p t h", h=2)[:, :, h]
                    ins = dve.tensor_tensor(blocks_of((diag, acc)[h][:, :]), ident_4, column_4(inv), ALU.mult)
                ins.then_inc(kdiag_done, 1)

            def k_normed(a):
                dve.wait_ge(kbc_done, a + 1)
                dve.scalar_tensor_tensor(t1[:, :], t1[:, :], gain("ev_k" if a < 4 else "od_k", 0), ps_misc[:, :],
                                         ALU.mult, ALU.mult).then_inc(kn_done, 1)

            def k_low(a):
                dve.wait_ge(k_hi_done, a + 1)
                dve.tensor_tensor(k_lo[:, a % 2, :], t1[:, :], k_hi[:, a % 2, :].bitcast(F32), ALU.subtract).then_inc(k_lo_done, 1)

            def v_low(a):
                dve.wait_ge(v_hi_done, a + 1)
                v = ps_misc[:, :].rearrange("p (t f) -> p t f", f=P)
                for h in range(2):
                    w = slice(2 * h * HD, 2 * h * HD + HD)
                    ins = dve.tensor_tensor(v_lo[:, a % 2, :, w], v[:, :, h * HD:(h + 1) * HD],
                                            v_hi[:, a % 2, :, w].bitcast(F32), ALU.subtract)
                ins.then_inc(v_lo_done, 1)

            def row_bias(a, r):
                R, h, t = 8 * a + r, r // 4, r % 4
                n = (t + 1) * P
                p = probs[:, R % 2, 0:n]
                dve.wait_ge(scaled_q_done, R + 1)
                if a >= 4 and t:
                    dve.tensor_tensor(p, p, keep(t), ALU.add).then_inc(masked_done, 1)
                    dve.wait_ge(masked_done, 3 * (2 * (a - 4) + h) + t)
                if R == 0:
                    dve.wait_ge(bias_landed, 16)
                if R >= 2:
                    dve.wait_ge(exp_done, R - 1)
                dve.tensor_tensor_reduce(p, p, bias_t[:, 2 * (a % 4) + h, T - n:T], -1.0, 3e38, ALU.add, ALU.min,
                                         negmax[:, R % 2:R % 2 + 1]).then_inc(biased_done, 1)

            def row_norm(a, r):
                R, n = 8 * a + r, (r % 4 + 1) * P
                p, inv = probs[:, R % 2, 0:n], rowinv[:, R % 2:R % 2 + 1]
                dve.wait_ge(exp_done, R + 1)
                if R >= 2:
                    dve.wait_ge(prob_done, R - 1)
                dve.reciprocal(inv, rowsum[:, R % 2:R % 2 + 1]).then_inc(rowinv_done, 1)
                dve.wait_ge(rowinv_done, R + 1)
                dve.tensor_scalar(p, p, inv, None, ALU.mult).then_inc(prob_done, 1)

            def pt_low(a, r):
                R, n = 8 * a + r, r % 4 + 1
                w = slice((n - 1) * P, n * P)
                dve.wait_ge(pt_hi_done, R + 1)
                dve.tensor_tensor(pt_lo[:, 0:n, w], ps_t[:, R % 2, 0:n * P].rearrange("p (j t) -> p j t", t=P),
                                  pt_hi[:, 0:n, w].bitcast(F32), ALU.subtract).then_inc(pt_lo_done, 1)

            def y_low(a):
                dve.wait_ge(y_hi_done, a + 1)
                w = slice((4 + a % 4) * T, (5 + a % 4) * T)
                dve.tensor_tensor(a_lo[:, w], ps_y[:, :], a_hi[:, w].bitcast(F32), ALU.subtract).then_inc(y_lo_done, 1)

            def attend(a, p, first):
                if p == 0 and not first:
                    y_low(a - 1)
                for r in (2 * p - 2, 2 * p - 1):
                    if r >= 0:
                        pt_low(a, r)
                if p < 4:
                    row_bias(a, 2 * p)
                    row_bias(a, 2 * p + 1)

            def attend_end(a, p):
                if p < 4:
                    row_norm(a, 2 * p)
                    row_norm(a, 2 * p + 1)

            def pair_read(a, u, n):
                if u < 3:
                    (q_scaled, k_scaled, v_scaled)[u](a, n)

            def pair_in(a, u):
                if u == 0:
                    q_low(a)
                if u == 2:
                    head_inv(a)
                if u == 3:
                    v_low(a)
                if u == 4:
                    k_normed(a)
                    if 0 < a < 4:
                        lru_low(a - 1)
                    k_low(a)

            def lru_in(j, n):
                dve.wait_ge(unit_done, n + 1)
                dve.wait_ge(pad_done, 1)
                if j:
                    dve.wait_ge(conv_done, 4 * j)
                dve.tensor_tensor(xr_pad[:, TAPS - 1:TAPS - 1 + T], ps_unit[:, n % 2, :], rstd[:, :], ALU.mult).then_inc(unit_read, 1)

            def lru_conv(j, n):
                dve.wait_ge(unit_read, n + 1)
                if j:
                    dve.wait_ge(ix_done, j)
                for k in range(TAPS):
                    src, w = xr_pad[:, k:k + T], gain("conv_w", TAPS * j + k)
                    if k == 0:
                        dve.tensor_scalar(xc, src, w, gain("conv_b", j), ALU.mult, ALU.add).then_inc(conv_done, 1)
                    else:
                        dve.scalar_tensor_tensor(xc, src, w, xc, ALU.mult, ALU.add).then_inc(conv_done, 1)
                    dve.wait_ge(conv_done, 4 * j + k + 1)

            def gate_in(j, n):
                dve.wait_ge(unit_done, n + 1)
                if j >= 2:
                    dve.wait_ge(ly_done, j - 1)
                dve.tensor_tensor(gelu[j % 2], ps_unit[:, n % 2, :], rstd[:, :], ALU.mult).then_inc(unit_read, 1)

            def lru_low(j):
                dve.wait_ge(l_hi_done, j + 1)
                dve.tensor_tensor(a_lo[:, j * T:(j + 1) * T], hh, a_hi[:, j * T:(j + 1) * T].bitcast(F32), ALU.subtract).then_inc(l_lo_done, 1)

            def lru(j, u, n):
                if 0 <= j < 4:
                    if u == 1:
                        dve.wait_ge(sqa_done, j + 1)
                        dve.scalar_tensor_tensor(half[:, :], hh, 1.0, half[:, :], ALU.add, ALU.mult).then_inc(mult2_done, 1)
                    if u == 2:
                        dve.wait_ge(sig_i_done, j + 1)
                        dve.tensor_tensor(ri, ri, xc, ALU.mult).then_inc(ix_done, 1)
                    if u == 3:
                        dve.wait_ge(mult_done, j + 1)
                        dve.wait_ge(ix_done, j + 1)
                        dve.tensor_tensor(ri, ri, half[:, :], ALU.mult).then_inc(u_done, 1)
                        dve.wait_ge(u_done, j + 1)
                        dve.wait_ge(mult2_done, j + 1)
                        dve.tensor_tensor_scan(hh, ra, ri, 0.0, ALU.mult, ALU.add).then_inc(scan_done, 1)
                        dve.wait_ge(scan_done, j + 1)
                        dve.wait_ge(gelu_done, j + 1)
                        dve.tensor_tensor(hh, hh, gelu[j % 2], ALU.mult).then_inc(ly_done, 1)
                    if j == 3 and u == 4:
                        lru_low(3)
                if j < 3:
                    if u == 3:
                        lru_conv(j + 1, n)
                    if u == 4:
                        dve.wait_ge(xc_hi_done, j + 2)
                        dve.tensor_tensor(xc_lo[:, :], xc, xc_hi[:, :].bitcast(F32), ALU.subtract).then_inc(xc_lo_done, 1)

            def mix_out(i, a):
                n = out_base(i)
                for u in range(5):
                    if PHASES[i] == "odd" and u == 0:
                        conv_norm(5)
                    attend(a, u, False)
                    attend_end(a, u)
                    if u < SPLIT_TILES:
                        dve.wait_ge(unit_done, n + u + 1)
                        dve.tensor_tensor(xt_tile(u), xt_tile(u), ps_unit[:, (n + u) % 2, :], ALU.add).then_inc(unit_read, 1)
                        m = n + u + 2
                        split_lo(m, m % RAW, m % 2)
                    if PHASES[i] == "even":
                        lru(3, u, n)
                y_low(a)
                dve.wait_ge(unit_read, n + SPLIT_TILES)
                for d in range(KT):
                    dve.wait_ge(*late(i, d, late_done, unit_done))
                    dve.tensor_tensor(xt_tile(d), xt_tile(d), late_bank(i, d), ALU.add).then_inc(late(i, d, late_read, unit_read)[0], 1)
                    if d >= SPLIT_TILES - 1:
                        m = n + d + 3
                        split_lo(m, m % RAW, m % 2)
                        for e in X_AFTER[d - SPLIT_TILES + 1]:
                            dve.wait_ge(*late(i, e, late_read, unit_read))
                            split_x(i + 1, e)

            def even(i):
                n0 = UNIT_BASE[i]
                dve.wait_ge(bd_lo_done, 1)
                dve.wait_ge(skewed, 16)
                dve.memset(xr_pad[:, 0:TAPS - 1], 0.0).then_inc(pad_done, 1)
                for it in range(4):
                    for u in range(5):
                        n = n0 + 5 * it + u
                        if it == 0 and u == 0:
                            split_lo(n + 2, (n + 2) % RAW, (n + 2) % 2)
                            norm_diag(i)
                            norm_rstd(i)
                            dve.wait_ge(half_done, i + 1)
                        pair_read(it, u, n)
                        if u == 3:
                            lru_in(it, n)
                        if u == 4:
                            gate_in(it, n)
                        if it or u:
                            split_lo(n + 2, (n + 2) % RAW, (n + 2) % 2)
                        if it:
                            attend(it - 1, u, it == 1)
                        pair_in(it, u)
                        if it:
                            attend_end(it - 1, u)
                        lru(it - 1, u, n)
                mix_out(i, 3)

            def keep(t):
                start = (2, 5, 9)[t - 1] - (t + 1)
                return isc[:, start * P:(start + t + 1) * P]

            def index_row(q):
                t, h = 1 + q // HEADS, q % HEADS
                w = wi[:, t * HEADS + h:t * HEADS + h + 1]
                dve.wait_ge(relu_done, q + 1)
                r = relu[q % 2][:, 0:(t + 1) * P]
                if h == 0:
                    dve.tensor_scalar(keep(t), r, w, None, ALU.mult).then_inc(isc_done, 1)
                else:
                    dve.wait_ge(isc_done, q)
                    dve.scalar_tensor_tensor(keep(t), r, w, keep(t), ALU.mult, ALU.add).then_inc(isc_done, 1)

            def cut_round(c):
                t, r = 1 + c // 16, c % 16
                if r == 0:
                    dve.wait_ge(isc_done, HEADS * t)
                    dve.wait_ge(causal_done, 2)
                    diag_part = keep(t)[:, t * P:(t + 1) * P]
                    dve.tensor_tensor(diag_part, diag_part, causal, ALU.add).then_inc(sel_done, 1)
                    dve.wait_ge(sel_done, 2 * t - 1)
                else:
                    dve.wait_ge(cut_done, c)
                dve.max(top8, keep(t)).then_inc(top_done, 1)
                tap(c)
                dve.wait_ge(top_done, c + 1)
                dve.match_replace(keep(t), top8, keep(t), -3e38).then_inc(cut_done, 1)
                if r == 15:
                    dve.wait_ge(cut_done, c + 1)
                    dve.tensor_scalar(keep(t), keep(t), -2e38, NEG, ALU.is_gt, ALU.mult).then_inc(sel_done, 1)
                    dve.wait_ge(sel_done, 2 * t)

            def tap(c):
                j, k = c // VE_TAPS, TE_TAPS + c % VE_TAPS
                src, w = c_pad[j][:, k:k + T], gain("dw_w", DW_TAPS * j + k)
                if k == TE_TAPS:
                    dve.wait_ge(glu_done, j + 1)
                    dve.tensor_scalar(cv[j], src, w, gain("dw_b", j), ALU.mult, ALU.add).then_inc(dw_done, 1)
                else:
                    dve.wait_ge(dw_done, c)
                    dve.scalar_tensor_tensor(cv[j], src, w, cv[j], ALU.mult, ALU.add).then_inc(dw_done, 1)

            def conv_low(j):
                at = j % 2 * 2 * T
                w = slice(at, at + T + DW_TAPS - 1)
                dve.wait_ge(c_hi_done, j + 1)
                dve.tensor_tensor(a_lo[:, w], c_pad[j], a_hi[:, w].bitcast(F32), ALU.subtract).then_inc(c_lo_done, 1)

            def conv_add(j, c, n):
                dve.wait_ge(unit_done, n + 1)
                if c == 0:
                    dve.wait_ge(dw_done, VE_TAPS * (j + 1))
                else:
                    dve.wait_ge(unit_read, n)
                dve.tensor_tensor(cv[j], cv[j], ps_unit[:, n % 2, :], ALU.add).then_inc(unit_read, 1)

            def conv_norm(u):
                def step(k, ins):
                    ins.then_inc(ln_chain, 1)
                    dve.wait_ge(ln_chain, k)

                if u == 0:
                    step(1, dve.tensor_tensor(branch_sum, cv[0], cv[1], ALU.add))
                    step(2, dve.tensor_tensor(branch_sum, branch_sum, cv[2], ALU.add))
                    dve.tensor_tensor(branch_sum, branch_sum, cv[3], ALU.add).then_inc(ln_add_done, 1)
                if u == 1:
                    dve.wait_ge(mean_mm, 1)
                    for c in range(4):
                        dve.scalar_tensor_tensor(cv[c], ps_misc[:, :], -1.0 / (4 * P), cv[c], ALU.mult, ALU.add).then_inc(cen_done, 1)
                if u == 2:
                    dve.wait_ge(cen_sq_done, 4)
                    step(3, dve.tensor_tensor(branch_sum, squares[0], squares[1], ALU.add))
                    step(4, dve.tensor_tensor(branch_sum, branch_sum, squares[2], ALU.add))
                    dve.tensor_tensor(branch_sum, branch_sum, squares[3], ALU.add).then_inc(ln_add_done, 1)
                if u == 3:
                    dve.wait_ge(ln_std_done, 1)
                    dve.reciprocal(rcol[:, :], small[:, 1:1 + TT]).then_inc(ln_rcol_done, 1)
                    dve.wait_ge(ln_rcol_done, 1)
                    dve.tensor_tensor(blocks_of(branch_diag), ident_4, column_4(rcol[:, 0:TT]), ALU.mult).then_inc(ln_diag_done, 1)
                if u == 4:
                    dve.wait_ge(ln_inv_done, 1)
                    for c in range(4):
                        dve.scalar_tensor_tensor(cv[c], cv[c], gain("ln_g", c), branch_inv, ALU.mult, ALU.mult).then_inc(scaled_done, 1)
                if u == 5:
                    for c in range(4):
                        w = slice(c * T, (c + 1) * T)
                        dve.wait_ge(l_hi_done, 4 + c + 1)
                        dve.tensor_tensor(a_lo[:, w], cv[c], a_hi[:, w].bitcast(F32), ALU.subtract).then_inc(l_lo_done, 1)

            def odd(i):
                n0 = UNIT_BASE[i]
                for j in range(4):
                    dve.memset(c_pad[j][:, 0:DW_TAPS - 1], 0.0).then_inc(pad_done, 1)
                for u in range(IDX_IN):
                    n = n0 + u
                    if u == 0:
                        split_lo(n + 2, (n + 2) % RAW, (n + 2) % 2)
                        norm_diag(i)
                        norm_rstd(i)
                        dve.wait_ge(half_done, i + 1)
                    dve.wait_ge(unit_done, n + 1)
                    if u >= 2:
                        dve.wait_ge(qi_lo_done, u - 1)
                    dve.tensor_tensor((t1 if u else t0)[:, :], ps_unit[:, n % 2, :], rstd[:, :], ALU.mult).then_inc(unit_read, 1)
                    if u:
                        split_lo(n + 2, (n + 2) % RAW, (n + 2) % 2)
                        w = slice((3 + u) * T, (4 + u) * T)
                        dve.wait_ge(qi_hi_done, u)
                        dve.tensor_tensor(a_lo[:, w], t1[:, :], a_hi[:, w].bitcast(F32), ALU.subtract).then_inc(qi_lo_done, 1)
                    else:
                        dve.wait_ge(ki_hi_done, 1)
                        dve.tensor_tensor(ki_lo[0:HD, :], t0[0:HD, :], ki_hi[0:HD, :].bitcast(F32), ALU.subtract).then_inc(ki_lo_done, 1)
                for m in range(GLU_IN):
                    n = n0 + IDX_IN + m
                    dve.wait_ge(unit_done, n + 1)
                    if m == 0:
                        dve.wait_ge(qi_lo_done, 4)
                    elif m >= 2:
                        dve.wait_ge(glu_done, m // 2)
                    dve.tensor_tensor((t1, t2)[m % 2][:, :], ps_unit[:, n % 2, :], rstd[:, :], ALU.mult).then_inc(unit_read, 1)
                    split_lo(n + 2, (n + 2) % RAW, (n + 2) % 2)
                    if m == 0:
                        dve.wait_ge(wi_turned, 1)
                        w = ps_misc[:, :].rearrange("p (t f) -> p t f", f=P)[:, :, HD:HD + HEADS]
                        dve.tensor_scalar(wi.rearrange("p (t h) -> p t h", h=HEADS), w, (HD ** -0.5) * (HEADS ** -0.5), None,
                                          ALU.mult).then_inc(wi_done, 1)
                        dve.wait_ge(wi_done, 1)
                    if m < 4:
                        for q in range(6 * m, 6 * m + 6):
                            index_row(q)
                    if m % 2:
                        dve.wait_ge(glu_sig_done, m // 2 + 1)
                        dve.tensor_tensor(c_pad[m // 2][:, DW_TAPS - 1:], t1[:, :], t2[:, :], ALU.mult).then_inc(glu_done, 1)
                    if m:
                        for c in range(4 * m - 4, 4 * m):
                            cut_round(c)
                    if m == 4 or m == 5:
                        conv_low(m - 4)
                for k, n in enumerate(range(n0 + IDX_IN + GLU_IN, n0 + ODD_FIRST)):
                    conv_add(k // CONV_UNITS, k % CONV_UNITS, n)
                    split_lo(n + 2, (n + 2) % RAW, (n + 2) % 2)
                    for c in range(28 + 4 * k, 32 + 4 * k):
                        cut_round(c)
                for it in range(4):
                    for u in range(5):
                        n = n0 + ODD_BASE[it] + u
                        if it == 0 and u == 0:
                            dve.wait_ge(glu_done, 4)
                        if u < 3:
                            pair_read(4 + it, u, n)
                        elif u < ODD_IN[it]:
                            conv_add(it + 1, u - 3, n)
                        if u < ODD_IN[it]:
                            split_lo(n + 2, (n + 2) % RAW, (n + 2) % 2)
                        if it == 0 and u == 0:
                            for c in range(44, 48):
                                cut_round(c)
                        if it == 3 and u == 1:
                            conv_norm(u)
                        if it:
                            attend(4 + it - 1, u, it == 1)
                        if u == 1 and it in (1, 2):
                            conv_low(it + 1)
                        pair_in(4 + it, u)
                        if it:
                            attend_end(4 + it - 1, u)
                        if it == 3 and u in (1, 2):
                            conv_norm(u + 1)
                        if it == 0 and u:
                            for c in range(45 + 3 * u, 48 + 3 * u):
                                tap(c)
                        if it == 2 and u == 4:
                            dve.wait_ge(unit_read, n + 1)
                            conv_norm(0)
                        if it == 3 and u == 3:
                            conv_norm(4)
                mix_out(i, 7)

            dve.wait_ge(const_done, 12)
            dve.wait_ge(vec_landed, 16)
            for d in range(KT):
                if d < 2:
                    split_lo(d, d, d)
                dve.wait_ge(x_landed[d], 16)
                split_x(0, d)
            dve.wait_ge(sp_done, 1)
            dve.reciprocal(sp[:, 8:12], sp[:, 12:16]).then_inc(sp_inv_done, 1)
            for i, phase in enumerate(PHASES):
                {"ffn": ffn, "even": even, "odd": odd}[phase](i)


def columns(w, start, tiles):
    part = w[:, start:start + tiles * P]
    return part.reshape(KT, P, tiles, P).transpose(2, 1, 0, 3).reshape(tiles, P, UNIT)


def ffn_units(w_gate, w_up, w_down):
    gate_up = np.stack([columns(w_gate, 0, FT), columns(w_up, 0, FT)], 1).reshape(2 * FT, P, UNIT)
    down = w_down.reshape(FT, P, KT, P).transpose(2, 1, 0, 3)
    parts, f = [], 0
    for tiles in GROUPS:
        parts.append(gate_up[2 * f:2 * (f + tiles)])
        group = np.zeros((KT, P, UNIT), np.float32)
        group[:, :, :tiles * P] = down[:, :, f:f + tiles].reshape(KT, P, tiles * P)
        parts.append(group)
        f += tiles
    return parts


def out_units(w, phase):
    ks = list(EARLY[phase] + LATE[phase])
    blocks = columns(w, 0, KT).reshape(KT, P, KT, P)[:, :, ks]
    first = np.zeros((SPLIT_TILES + 1, P, KT, P), np.float32)
    n = len(EARLY[phase])
    first[:SPLIT_TILES, :, :n] = blocks[:SPLIT_TILES, :, :n]
    for d in range(SPLIT_TILES):
        first[-1, :, d * (KT - n):(d + 1) * (KT - n)] = blocks[d, :, n:]
    return [first.reshape(SPLIT_TILES + 1, P, UNIT), blocks[SPLIT_TILES:].reshape(-1, P, UNIT)]


def tap_units(w, i):
    units = np.zeros((CONV_UNITS, P, KT, P), np.float32)
    for k in range(TE_TAPS):
        units[k // KT, np.arange(P), k % KT, np.arange(P)] = w[k, i * P:(i + 1) * P]
    return [units.reshape(CONV_UNITS, P, UNIT)]


def by_tile(v):
    return v.reshape(-1, P).T


def lay_out(a):
    even, odd = a["ev_w_in"][0], a["od_w_in"][0]
    pair = lambda w, starts, i: [columns(w, s + i * P, 1) for s in starts]
    units = []
    units += ffn_units(a["ffn1_w_gate"][0], a["ffn1_w_up"][0], a["ffn1_w_down"][0])
    for i in range(4):
        units += pair(even, (1024, 1536, 2048, 512, 0), i)
    units += out_units(a["ev_w_out"][0], "even")
    units += ffn_units(a["ffn2_w_gate"][0], a["ffn2_w_up"][0], a["ffn2_w_down"][0])
    units += ffn_units(a["ffn1_w_gate"][1], a["ffn1_w_up"][1], a["ffn1_w_down"][1])
    kiwi = np.zeros((D, P), np.float32)
    kiwi[:, :HD + HEADS] = odd[:, 3072:3072 + HD + HEADS]
    units.append(columns(kiwi, 0, 1))
    units.append(columns(odd, 2560, 4))
    for i in range(4):
        units += pair(odd, (0, 512), i)
    for i in range(2):
        units += tap_units(a["od_dw_w"][0], i)
    for i in range(4):
        units += pair(odd, (1024, 1536, 2048), i)
        if ODD_IN[i] > 3:
            units += tap_units(a["od_dw_w"][0], i + 1)
    units += out_units(a["od_w_out"][0], "odd")
    units += ffn_units(a["ffn2_w_gate"][1], a["ffn2_w_up"][1], a["ffn2_w_down"][1])
    w_stream = np.concatenate(units, 0)

    norms = [a["ffn1_norm"][0], a["mix_norm"][0], a["ffn2_norm"][0], a["ffn1_norm"][1], a["mix_norm"][1], a["ffn2_norm"][1]]
    twice = lambda v: np.concatenate([v, v])
    taps = lambda w: w.reshape(w.shape[0], 4, P).transpose(2, 1, 0).reshape(P, -1)
    vec = np.concatenate(
        [by_tile(v) for v in norms]
        + [taps(a["ev_conv_w"][0])] + [by_tile(a[n][0]) for n in ("ev_conv_b", "ev_ra_b", "ev_ix_b", "ev_lambda")]
        + [by_tile(twice(a["ev_q_norm"][0])), by_tile(twice(a["ev_k_norm"][0]))]
        + [taps(a["od_dw_w"][0])] + [by_tile(a[n][0]) for n in ("od_dw_b", "od_ln_g", "od_ln_b")]
        + [by_tile(twice(a["od_q_norm"][0])), by_tile(twice(a["od_k_norm"][0]))], 1)

    bd = np.zeros((P, 2, 4, P), np.float32)
    for g, name in enumerate(("ev_ra_w", "ev_ix_w")):
        for b in range(8):
            at = slice(b % 2 * 64, b % 2 * 64 + 64)
            bd[at, g, b // 2, at] = a[name][0, b]

    distance = np.arange(T - 1, -1, -1)
    large = 16 + (np.log(np.maximum(distance, 1) / 16) / np.log(128 / 16) * 16).astype(np.int64)
    bucket = np.where(distance < 16, distance, np.minimum(large, BUCKETS - 1))
    onehot = (np.arange(BUCKETS)[:, None] == bucket[None, :]).astype(np.float32)

    return {
        "xt_in": a["x"][0].T.reshape(KT, P, T),
        "w_stream": w_stream,
        "vec_in": vec,
        "bd_in": bd.reshape(P, UNIT),
        "relb_in": a["rel_bias"],
        "onehot_in": onehot,
        "ident_in": np.eye(P, dtype=np.float32),
    }


def kernel(**inputs):
    import concourse.bacc as bacc
    from concourse.bass_utils import run_bass_kernel_spmd

    arrays = {k: np.ascontiguousarray(v) for k, v in lay_out({k: np.asarray(v) for k, v in inputs.items()}).items()}
    nc = bacc.Bacc("TRN2", target_bir_lowering=False, num_devices=1, dynamic_dma_scratch_size=1024)
    args = [nc.dram_tensor(k + "_dram", v.shape, mybir.dt.from_np(v.dtype), kind="ExternalInput").ap() for k, v in arrays.items()]
    out = nc.dram_tensor("out_dram", (KT, P, T), F32, kind="ExternalOutput").ap()
    build(nc, *args, out)
    r = run_bass_kernel_spmd(nc, [{k + "_dram": v for k, v in arrays.items()}], core_ids=[0])
    return r.results[0]["out_dram"].reshape(D, T).T[None]
```
